# Optimizing a Trainium2 kernel written in Bass

```python
import math
import jax
import jax.numpy as jnp
from jax import lax
import numpy as np

D_MODEL = 1024
BATCH = 1
SEQ = 256
DEPTH = 2
DEC_BATCH = 1
DEC_SEQ = 32
PAST_LEN = 256

CHUNK = 64
N_META = 16
ALPHA = (2 * DEPTH) ** 0.25
BETA = (8 * DEPTH) ** -0.25
LN_EPS = 1e-5
RMS_EPS = 1e-6
NEG_INF = -1e30
SEES_ALL = 2 ** 30

GLA_HEADS = 4
GLA_DK = 64
GLA_DV = 128
GLA_GATE_RANK = 16
GLA_TAU = 16.0
GLA_CHUNK = 64

MLA_HEADS = 8
MLA_Q_LORA = 256
MLA_KV_LORA = 128
MLA_NOPE = 64
MLA_ROPE = 32
MLA_V = 64
MLA_SCALE = (MLA_NOPE + MLA_ROPE) ** -0.5
ROPE_THETA = 10000.0
Q_BLOCK = 128

IN0_WIDTHS = (GLA_HEADS * GLA_DK, GLA_HEADS * GLA_DK, GLA_HEADS * GLA_DV, GLA_HEADS * GLA_DV,
              GLA_GATE_RANK, MLA_Q_LORA, MLA_KV_LORA, MLA_ROPE)
D_IN0 = sum(IN0_WIDTHS)
D_MIX0 = GLA_HEADS * GLA_DV + MLA_HEADS * MLA_V

POOL_WINDOWS = (2, 4, 8, 16)
POOL_GROUP = D_MODEL // len(POOL_WINDOWS)
POOL_MAX = 16

N_EXPERTS = 64
TOP_K = 8
N_GROUPS = 8
TOPK_GROUPS = 4
D_EXPERT = 256
ROUTED_SCALE = 2.5
EXPERT_BLOCK = 128

kernel_name = 'hybrid_gla_mla_pool_moe_stream'

def layer_norm(x, g, b):
    xf = x.astype(jnp.float32)
    mu = jnp.mean(xf, axis=-1, keepdims=True)
    var = jnp.mean(jnp.square(xf - mu), axis=-1, keepdims=True)
    return ((xf - mu) * lax.rsqrt(var + LN_EPS) * g + b).astype(x.dtype)

def rms_norm(x, g):
    xf = x.astype(jnp.float32)
    return (xf * lax.rsqrt(jnp.mean(jnp.square(xf), axis=-1, keepdims=True) + RMS_EPS) * g).astype(x.dtype)

def rope(x, pos):
    half = x.shape[-1] // 2
    inv = ROPE_THETA ** (-jnp.arange(half, dtype=jnp.float32) / half)
    ang = pos.astype(jnp.float32)[:, None] * inv
    cos, sin = jnp.cos(ang), jnp.sin(ang)
    xf = x.astype(jnp.float32)
    x1, x2 = xf[..., :half], xf[..., half:]
    return jnp.concatenate([x1 * cos - x2 * sin, x1 * sin + x2 * cos], axis=-1).astype(x.dtype)

def gla_recurrence(q, k, v, lg, s0):
    B, H, S, _ = q.shape
    n = -(-S // GLA_CHUNK)
    pad = n * GLA_CHUNK - S

    def to_chunks(t):
        t = jnp.pad(t, ((0, 0), (0, 0), (0, pad), (0, 0)))
        return jnp.moveaxis(t.reshape(B, H, n, GLA_CHUNK, t.shape[-1]), 2, 0)

    causal = jnp.tril(jnp.ones((GLA_CHUNK, GLA_CHUNK), dtype=bool))

    def step(s, inp):
        qc, kc, vc, gc = inp
        b = jnp.cumsum(gc, axis=2)
        o_inter = jnp.einsum('bhtd,bhdv->bhtv', qc * jnp.exp(b), s)
        diff = b[:, :, :, None, :] - b[:, :, None, :, :]
        decay = jnp.exp(jnp.where(causal[:, :, None], diff, -jnp.inf))
        att = jnp.einsum('bhtd,bhsd,bhtsd->bhts', qc, kc, decay)
        o = o_inter + jnp.einsum('bhts,bhsv->bhtv', att, vc)
        b_last = b[:, :, -1:, :]
        s = jnp.exp(b_last[:, :, 0, :])[..., None] * s + jnp.einsum('bhsd,bhsv->bhdv', kc * jnp.exp(b_last - b), vc)
        return s, o

    s, o = lax.scan(step, s0, (to_chunks(q), to_chunks(k), to_chunks(v), to_chunks(lg)))
    o = jnp.moveaxis(o, 0, 2).reshape(B, H, n * GLA_CHUNK, v.shape[-1])[:, :, :S]
    return o, s

def mla_attention(q_lat, q_rope, q_chunk, k_lat, k_rope, k_chunk):
    B, H, Sq, C = q_lat.shape
    qb = min(Q_BLOCK, Sq)
    nb = -(-Sq // qb)
    pad = nb * qb - Sq

    def blocks(t):
        t = jnp.pad(t, ((0, 0), (0, 0), (0, pad), (0, 0)))
        return jnp.moveaxis(t.reshape(B, H, nb, qb, t.shape[-1]), 2, 0)

    qch = jnp.pad(q_chunk, (0, pad), constant_values=SEES_ALL).reshape(nb, qb)

    def one_block(args):
        ql, qr, qc = args
        s = (jnp.einsum('bhqc,bkc->bhqk', ql, k_lat) + jnp.einsum('bhqr,bkr->bhqk', qr, k_rope)).astype(jnp.float32) * MLA_SCALE
        s = jnp.where(k_chunk[None, :] <= qc[:, None], s, NEG_INF)
        p = jax.nn.softmax(s, axis=-1).astype(k_lat.dtype)
        return jnp.einsum('bhqk,bkc->bhqc', p, k_lat)

    o = lax.map(one_block, (blocks(q_lat), blocks(q_rope), qch))
    return jnp.moveaxis(o, 0, 2).reshape(B, H, nb * qb, C)[:, :, :Sq]

def hybrid_mixer(x, q_pos, q_chunk, gla_s0, past_ckv, past_krope, past_chunk,
                 w_in0, gla_w_g2, gla_b_g, gla_norm_g, mla_q_norm_g, mla_kv_norm_g,
                 mla_w_uq, mla_w_uk, mla_w_uv, w_out0):
    B, S, _ = x.shape
    h = x @ w_in0
    offs, acc = [], 0
    for w in IN0_WIDTHS[:-1]:
        acc += w
        offs.append(acc)
    q, k, v, r, a, cq, ckv, kr = jnp.split(h, offs, axis=-1)

    def heads(t, d):
        return t.reshape(B, S, GLA_HEADS, d).transpose(0, 2, 1, 3)
    lg = jax.nn.log_sigmoid((a @ gla_w_g2 + gla_b_g).astype(jnp.float32)) / GLA_TAU
    o_gla, s_gla = gla_recurrence(heads(q, GLA_DK).astype(jnp.float32) * GLA_DK ** -0.5,
                                  heads(k, GLA_DK).astype(jnp.float32),
                                  heads(v, GLA_DV).astype(jnp.float32),
                                  heads(lg, GLA_DK), gla_s0.astype(jnp.float32))
    o_gla = rms_norm(o_gla, gla_norm_g).transpose(0, 2, 1, 3).reshape(B, S, GLA_HEADS * GLA_DV)
    o_gla = o_gla.astype(x.dtype) * jax.nn.silu(r)

    qh = (rms_norm(cq, mla_q_norm_g) @ mla_w_uq).reshape(B, S, MLA_HEADS, MLA_NOPE + MLA_ROPE).transpose(0, 2, 1, 3)
    q_nope, q_rope = qh[..., :MLA_NOPE], rope(qh[..., MLA_NOPE:], q_pos)
    ckv = rms_norm(ckv, mla_kv_norm_g)
    kr = rope(kr, q_pos)
    k_lat = jnp.concatenate([past_ckv.astype(ckv.dtype), ckv], axis=1)
    k_rope = jnp.concatenate([past_krope.astype(kr.dtype), kr], axis=1)
    k_chunk = jnp.concatenate([past_chunk, q_chunk])
    q_lat = jnp.einsum('bhqn,chn->bhqc', q_nope, mla_w_uk)
    o_lat = mla_attention(q_lat, q_rope, q_chunk, k_lat, k_rope, k_chunk)
    o_mla = jnp.einsum('bhqc,chv->bqhv', o_lat, mla_w_uv).reshape(B, S, MLA_HEADS * MLA_V)

    out = jnp.concatenate([o_gla, o_mla], axis=-1) @ w_out0
    return out, s_gla.astype(gla_s0.dtype), ckv, kr

def pool_mixer(x, past, pool_w, pool_scale):
    P, S = past.shape[1], x.shape[1]
    xp = jnp.concatenate([past.astype(x.dtype), x], axis=1)
    cs = jnp.pad(jnp.cumsum(xp.astype(jnp.float32), axis=1), ((0, 0), (1, 0), (0, 0)))
    idx = P + jnp.arange(S)
    outs = []
    for g, w in enumerate(POOL_WINDOWS):
        sl = slice(g * POOL_GROUP, (g + 1) * POOL_GROUP)
        lo = jnp.maximum(idx + 1 - w, 0)
        cnt = (idx + 1 - lo).astype(jnp.float32)
        mean = (cs[:, idx + 1, sl] - cs[:, lo, sl]) / cnt[None, :, None]
        mix = (mean - x[..., sl].astype(jnp.float32)).astype(x.dtype)
        outs.append(mix @ pool_w[g])
    y = jnp.concatenate(outs, axis=-1) * pool_scale
    return y, xp[:, xp.shape[1] - (POOL_MAX - 1):]

def routed_experts(x2, idx, wts, w_gate, w_up, w_down):
    T, D = x2.shape
    A = T * TOP_K
    flat_e = idx.reshape(A)
    flat_tok = jnp.arange(A, dtype=jnp.int32) // TOP_K
    order = jnp.argsort(flat_e)
    e_sorted = flat_e[order]
    counts = jnp.zeros((N_EXPERTS,), jnp.int32).at[flat_e].add(1)
    padded = (counts + EXPERT_BLOCK - 1) // EXPERT_BLOCK * EXPERT_BLOCK
    start = jnp.cumsum(counts) - counts
    pad_end = jnp.cumsum(padded)
    pad_start = pad_end - padded
    dest = pad_start[e_sorted] + (jnp.arange(A, dtype=jnp.int32) - start[e_sorted])
    n_blocks = -(-A // EXPERT_BLOCK) + N_EXPERTS
    P = n_blocks * EXPERT_BLOCK
    tok_buf = jnp.full((P,), T, jnp.int32).at[dest].set(flat_tok[order])
    gate_buf = jnp.zeros((P,), jnp.float32).at[dest].set(wts.reshape(A)[order])
    blk_e = jnp.minimum(jnp.searchsorted(pad_end, jnp.arange(n_blocks, dtype=jnp.int32) * EXPERT_BLOCK, side='right'), N_EXPERTS - 1)
    x_pad = jnp.concatenate([x2, jnp.zeros((1, D), x2.dtype)], axis=0)

    def body(acc, blk):
        toks, gates, e = blk
        xb = x_pad[toks]
        hb = jax.nn.silu(xb @ w_gate[e]) * (xb @ w_up[e])
        return acc.at[toks].add((hb @ w_down[e]).astype(jnp.float32) * gates[:, None]), None

    acc, _ = lax.scan(body, jnp.zeros((T + 1, D), jnp.float32),
                      (tok_buf.reshape(n_blocks, EXPERT_BLOCK), gate_buf.reshape(n_blocks, EXPERT_BLOCK), blk_e))
    return acc[:T]

def moe_layer(x, router_w, router_b, w_gate, w_up, w_down, sh_gate, sh_up, sh_down):
    B, S, D = x.shape
    T = B * S
    x2 = x.reshape(T, D)
    scores = jax.nn.sigmoid((x2 @ router_w).astype(jnp.float32))
    biased = scores + router_b.astype(jnp.float32)
    grouped = biased.reshape(T, N_GROUPS, N_EXPERTS // N_GROUPS)
    group_score = jnp.sum(lax.top_k(grouped, 2)[0], axis=-1)
    _, top_groups = lax.top_k(group_score, TOPK_GROUPS)
    group_ok = jnp.sum(jax.nn.one_hot(top_groups, N_GROUPS, dtype=jnp.float32), axis=1) > 0
    masked = jnp.where(group_ok[:, :, None], grouped, -jnp.inf).reshape(T, N_EXPERTS)
    _, idx = lax.top_k(masked, TOP_K)
    wts = jnp.take_along_axis(scores, idx, axis=1)
    wts = wts / jnp.sum(wts, axis=-1, keepdims=True) * ROUTED_SCALE
    routed = routed_experts(x2, idx, wts, w_gate, w_up, w_down)
    shared = (jax.nn.silu(x2 @ sh_gate) * (x2 @ sh_up)) @ sh_down
    return (routed.astype(x.dtype) + shared).reshape(B, S, D)

def setup_inputs(seed: int = 0) -> dict:
    key = jax.random.key(seed)
    ks = iter(jax.random.split(key, 40))
    D, E, F = D_MODEL, N_EXPERTS, D_EXPERT

    def nrm(shape, scale):
        return jax.random.normal(next(ks), shape, jnp.float32) * scale

    def gain(shape):
        return 1.0 + nrm(shape, 0.01)

    return {
        'x_prompt': nrm((BATCH, SEQ, D), 1.0),
        'x_sample': nrm((DEC_BATCH, DEC_SEQ, D), 1.0),
        'cache_mla_ckv': nrm((DEC_BATCH, N_META + PAST_LEN, MLA_KV_LORA), 1.0),
        'cache_mla_krope': nrm((DEC_BATCH, N_META + PAST_LEN, MLA_ROPE), 1.0),
        'state_gla': nrm((DEC_BATCH, GLA_HEADS, GLA_DK, GLA_DV), 0.5),
        'cache_pool': nrm((DEC_BATCH, POOL_MAX - 1, D), 1.0),
        'meta_tokens': nrm((N_META, D), 1.0),
        'w_in0': nrm((D, D_IN0), D ** -0.5),
        'gla_w_g2': nrm((GLA_GATE_RANK, GLA_HEADS * GLA_DK), GLA_GATE_RANK ** -0.5),
        'gla_b_g': nrm((GLA_HEADS * GLA_DK,), 0.1),
        'gla_norm_g': gain((GLA_DV,)),
        'mla_q_norm_g': gain((MLA_Q_LORA,)),
        'mla_kv_norm_g': gain((MLA_KV_LORA,)),
        'mla_w_uq': nrm((MLA_Q_LORA, MLA_HEADS * (MLA_NOPE + MLA_ROPE)), MLA_Q_LORA ** -0.5),
        'mla_w_uk': nrm((MLA_KV_LORA, MLA_HEADS, MLA_NOPE), MLA_KV_LORA ** -0.5),
        'mla_w_uv': nrm((MLA_KV_LORA, MLA_HEADS, MLA_V), MLA_KV_LORA ** -0.5),
        'w_out0': nrm((D_MIX0, D), BETA * D_MIX0 ** -0.5),
        'pool_w': nrm((len(POOL_WINDOWS), POOL_GROUP, POOL_GROUP), BETA * POOL_GROUP ** -0.5),
        'pool_scale': gain((D,)),
        'ln_g': gain((DEPTH, 2, D)),
        'ln_b': nrm((DEPTH, 2, D), 0.01),
        'moe_router_w': nrm((DEPTH, D, E), D ** -0.5),
        'moe_router_b': nrm((DEPTH, E), 0.01),
        'moe_w_gate': nrm((DEPTH, E, D, F), D ** -0.5),
        'moe_w_up': nrm((DEPTH, E, D, F), D ** -0.5),
        'moe_w_down': nrm((DEPTH, E, F, D), BETA * F ** -0.5),
        'moe_sh_gate': nrm((DEPTH, D, F), D ** -0.5),
        'moe_sh_up': nrm((DEPTH, D, F), D ** -0.5),
        'moe_sh_down': nrm((DEPTH, F, D), BETA * F ** -0.5),
    }

def reference(x_prompt, x_sample, cache_mla_ckv, cache_mla_krope, state_gla, cache_pool,
              meta_tokens, w_in0, gla_w_g2, gla_b_g, gla_norm_g, mla_q_norm_g, mla_kv_norm_g,
              mla_w_uq, mla_w_uk, mla_w_uv, w_out0, pool_w, pool_scale, ln_g, ln_b,
              moe_router_w, moe_router_b, moe_w_gate, moe_w_up, moe_w_down,
              moe_sh_gate, moe_sh_up, moe_sh_down):

    def trunk(x, q_pos, q_chunk, gla_s0, past_ckv, past_krope, past_chunk, pool_past):
        for layer in range(DEPTH):
            if layer % 2 == 0:
                out, s_gla, ckv, kr = hybrid_mixer(
                    x, q_pos, q_chunk, gla_s0, past_ckv, past_krope, past_chunk,
                    w_in0, gla_w_g2, gla_b_g, gla_norm_g, mla_q_norm_g, mla_kv_norm_g,
                    mla_w_uq, mla_w_uk, mla_w_uv, w_out0)
            else:
                out, pool_rows = pool_mixer(x, pool_past, pool_w, pool_scale)
            x = layer_norm(ALPHA * x + out, ln_g[layer, 0], ln_b[layer, 0])
            ffn = moe_layer(x, moe_router_w[layer], moe_router_b[layer], moe_w_gate[layer], moe_w_up[layer],
                            moe_w_down[layer], moe_sh_gate[layer], moe_sh_up[layer], moe_sh_down[layer])
            x = layer_norm(ALPHA * x + ffn, ln_g[layer, 1], ln_b[layer, 1])
        return x, ckv, kr, s_gla, pool_rows

    B, S, D = x_prompt.shape
    dt = x_prompt.dtype
    meta = jnp.broadcast_to(meta_tokens.astype(dt)[None], (B, N_META, D))
    xp = jnp.concatenate([meta, x_prompt], axis=1)
    p_pos = jnp.arange(N_META + S, dtype=jnp.int32)
    p_chunk = jnp.concatenate([jnp.full((N_META,), -1, jnp.int32), jnp.arange(S, dtype=jnp.int32) // CHUNK])
    y_full, p_ckv, p_kr, p_gla, p_pool = trunk(
        xp, p_pos, p_chunk,
        jnp.zeros((B, GLA_HEADS, GLA_DK, GLA_DV), dt),
        jnp.zeros((B, 0, MLA_KV_LORA), dt), jnp.zeros((B, 0, MLA_ROPE), dt),
        jnp.zeros((0,), jnp.int32), jnp.zeros((B, 0, D), dt))
    y_prompt = y_full[:, N_META:]

    past_len = cache_mla_ckv.shape[1] - N_META
    Sd = x_sample.shape[1]
    s_pos = N_META + past_len + jnp.arange(Sd, dtype=jnp.int32)
    s_chunk = (past_len + jnp.arange(Sd, dtype=jnp.int32)) // CHUNK
    past_chunk = jnp.concatenate([jnp.full((N_META,), -1, jnp.int32), jnp.arange(past_len, dtype=jnp.int32) // CHUNK])
    y_sample, s_ckv, s_kr, s_gla, s_pool = trunk(
        x_sample, s_pos, s_chunk, state_gla, cache_mla_ckv, cache_mla_krope, past_chunk, cache_pool)

    return (y_prompt, y_sample, p_ckv, p_kr, p_gla, p_pool, s_ckv, s_kr, s_gla, s_pool)


_drawn_inputs = setup_inputs


def setup_inputs(seed=0):
    import zlib

    import numpy as np

    out = dict(_drawn_inputs(seed))
    spreads = {}
    factors = {'gla_norm_g': 10.995,
     'mla_q_norm_g': 5.11,
     'mla_kv_norm_g': 5.674,
     'pool_scale': 20.149,
     'cache_mla_ckv': 8.0,
     'cache_mla_krope': 8.0}
    for name, (base, spread) in spreads.items():
        noise = np.random.default_rng([zlib.crc32(name.encode()), seed]).standard_normal(out[name].shape)
        drawn = base * np.exp(spread * noise) if base else spread * noise
        out[name] = jnp.asarray(drawn.astype(out[name].dtype))
    for name, factor in factors.items():
        out[name] = (out[name] * factor).astype(out[name].dtype)
    return out
```

```python
import math
from contextlib import ExitStack

import numpy as np

import concourse.bass as bass
from concourse import mybir

F32 = mybir.dt.float32
F32R = mybir.dt.float32r
I32 = mybir.dt.int32
ALU = mybir.AluOpType
ACT = mybir.ActivationFunctionType
AX = mybir.AxisListType

P = 128
D = 1024
SEQ, N_META, N_DEC, PAST = 256, 16, 32, 256
N_PROMPT = N_META + SEQ
N_KEYS_PAST = N_META + PAST
DEPTH = 2
ALPHA = float((2 * DEPTH) ** 0.25)
LN_EPS, RMS_EPS = 1e-5, 1e-6
NEG = -1e30

DK_SLICES = D // P
TILES = 3
ROWS = [128, 128, 64]
SAMPLE_ROW = 32
SAMPLE0 = 2 * P + SAMPLE_ROW
TAIL = N_PROMPT - 2 * P
T_COLS = 320
T_PAD = TILES * P

GH, GDK, GDV, GRANK = 4, 64, 128, 16
CHUNK = 64
TAU = 16.0
CHUNKS = [(0, 0, 64), (0, 64, 64), (1, 0, 64), (1, 64, 64), (2, 0, TAIL), (2, SAMPLE_ROW, N_DEC)]
LEVELS = 6

MH, QL_R, KVL, NOPE, ROPE, MV = 8, 256, 128, 64, 32, 64
MLA_SCALE = float((NOPE + ROPE) ** -0.5)
HALF = ROPE // 2
S_KEYS = 320

C_Q, C_K, C_V, C_R = 0, 256, 512, 1024
C_A, C_CQ, D_IN = 1536, 1552, 1968

E, FE, TOPG, NG, TOPK = 64, 256, 4, 8, 8
ROUTED_SCALE = 2.5
PAIRS = E // 2
GROUPS = PAIRS // 2
SLOTS = 64
ZEROED = 2 + 9 + 2
MIX_PARAMS = 11
MIX_STORES = 6 + 2 * GH
MAX_ROUNDS = -(-(N_PROMPT + N_DEC) // SLOTS)
BIG = 3e38
WIN = (2, 4, 8, 16)
PG = 256


def layout(widths):
    at, out = 0, {}
    for name, w in widths:
        out[name] = (at, at + w)
        at += w
    return out, at


CST, CST_W = layout([("ident", 128), ("before", 128), ("ones", 128), ("iota", SLOTS), ("valid", TILES),
                     ("thr", MAX_ROUNDS - 1), ("lower_group", NG * NG)])
MIX, MIX_W = layout([("gla", (LEVELS + 1) * 64), ("gla_s", LEVELS * 32), ("mask0", 144), ("mask1", N_PROMPT),
                     ("mask_s", S_KEYS), ("scan", T_COLS), ("cos", TILES * HALF), ("sin", TILES * HALF)])
BAND, BAND_W = layout([("own0", 4 * 128), ("own1", 4 * 128), ("prev1", 4 * 128), ("own2", 4 * 64),
                       ("prev2", 4 * 64), ("cache", 4 * 64)])


def constants():
    f = np.float32
    p = np.arange(P)
    cst = np.zeros((P, CST_W), f)
    put = lambda a, tab, n, v: a.__setitem__((slice(None), slice(*tab[n])), np.asarray(v, f).reshape(a.shape[0], -1))
    put(cst, CST, "ident", np.eye(P))
    put(cst, CST, "before", p[:, None] < p[None, :])
    put(cst, CST, "ones", np.ones((P, P)))
    put(cst, CST, "iota", np.tile(np.arange(SLOTS), (P, 1)))
    valid = np.ones((P, TILES))
    valid[:, 2] = (p < TAIL) | ((p >= SAMPLE_ROW) & (p < SAMPLE_ROW + N_DEC))
    put(cst, CST, "valid", valid)
    put(cst, CST, "thr", np.tile(SLOTS * np.arange(1, MAX_ROUNDS), (P, 1)))
    g = np.arange(NG)
    put(cst, CST, "lower_group", np.tile((g[None, :] < g[:, None]).reshape(1, -1), (P, 1)))

    mix = np.zeros((P, MIX_W), f)

    def level_masks(s, t):
        out = [s[:, None] == t[None, :]]
        for l in range(LEVELS):
            b, h = 2 << l, 1 << l
            out.append((s[:, None] // b == t[None, :] // b) & (s[:, None] % b < h) & (t[None, :] % b >= h))
        return np.stack(out, 1)

    put(mix, MIX, "gla", level_masks(p % 64, np.arange(64)))
    put(mix, MIX, "gla_s", level_masks(p % 32, np.arange(32))[:, :LEVELS])
    pos = np.arange(N_PROMPT)
    chunk = np.where(pos < N_META, -1, (pos - N_META) // CHUNK)
    seen = lambda q, k: np.where(chunk[:k][None, :] <= chunk[q][:, None], 0.0, NEG)
    put(mix, MIX, "mask0", seen(p, 144))
    put(mix, MIX, "mask1", seen(P + p, N_PROMPT))
    ks = np.arange(S_KEYS)
    put(mix, MIX, "mask_s", np.tile(np.where((ks >= N_KEYS_PAST) & (ks < SAMPLE0), NEG, 0.0), (P, 1)))
    cols = np.arange(T_COLS)
    put(mix, MIX, "scan", np.tile((cols % CHUNK != 0) & (cols != SAMPLE0), (P, 1)))
    tok = np.arange(T_PAD)
    tpos = np.where(tok < SAMPLE0, tok, N_META + PAST + tok - SAMPLE0).astype(f)
    inv = (f(10000.0) ** (-np.arange(HALF, dtype=f) / f(HALF))).astype(f)
    ang = (tpos[:, None] * inv).astype(f)
    put(mix, MIX, "cos", np.cos(ang).reshape(TILES, P, HALF).transpose(1, 0, 2))
    put(mix, MIX, "sin", np.sin(ang).reshape(TILES, P, HALF).transpose(1, 0, 2))

    band = np.zeros((P, BAND_W), f)
    full = np.zeros((4, T_PAD, T_PAD))
    cache = np.zeros((4, P, T_PAD))
    for gi, w in enumerate(WIN):
        for t in range(N_PROMPT):
            lo = max(t + 1 - w, 0)
            full[gi, lo:t + 1, t] = 1.0 / (t + 1 - lo)
            full[gi, t, t] -= 1.0
        for i in range(N_DEC):
            for j in range(i + 1 - w, i + 1):
                if j >= 0:
                    full[gi, SAMPLE0 + j, SAMPLE0 + i] += 1.0 / w
                else:
                    cache[gi, 15 + j, SAMPLE0 + i] = 1.0 / w
            full[gi, SAMPLE0 + i, SAMPLE0 + i] -= 1.0
    tr = lambda a: a.transpose(1, 0, 2)
    put(band, BAND, "own0", tr(full[:, 0:128, 0:128]))
    put(band, BAND, "own1", tr(full[:, 128:256, 128:256]))
    put(band, BAND, "prev1", tr(full[:, 0:128, 128:256]))
    put(band, BAND, "own2", tr(full[:, 256:384, 256:320]))
    put(band, BAND, "prev2", tr(full[:, 128:256, 256:320]))
    put(band, BAND, "cache", tr(cache[:, :, 256:320]))
    return cst, mix, band


class Banks:

    def __init__(self, nc, ctx, names):
        self.tile = [ctx.enter_context(nc.psum_tensor(f"bank{b}", [P, 512], F32)) for b in range(8)]
        self.filled = [ctx.enter_context(nc.semaphore(f"filled{b}")) for b in range(8)]
        self.emptied = [ctx.enter_context(nc.semaphore(f"emptied{b}")) for b in range(8)]
        self.order = names
        assert len(set(names)) == len(names)
        self.at = {n: (i % 8, i // 8) for i, n in enumerate(names)}
        self.next = 0

    def ap(self, name):
        return self.tile[self.at[name][0]]

    def open(self, pe, name):
        assert self.order[self.next] == name, (self.order[self.next], name)
        self.next += 1
        b, n = self.at[name]
        if n:
            pe.wait_ge(self.emptied[b], n)
        return self.tile[b]

    def full(self, eng, name):
        b, n = self.at[name]
        eng.wait_ge(self.filled[b], n + 1)
        return self.tile[b]

    def fill_sem(self, name):
        return self.filled[self.at[name][0]]

    def empty_sem(self, name):
        return self.emptied[self.at[name][0]]

    def copied(self, eng, name):
        b, n = self.at[name]
        eng.wait_ge(self.emptied[b], n + 1)

    def all_copied(self, eng, name):
        i = self.order.index(name)
        for b in range(8):
            n = sum(1 for k in range(i + 1) if k % 8 == b)
            if n:
                eng.wait_ge(self.emptied[b], n)


def bank_uses():
    u = [("xT", 0, i) for i in range(5)]
    u += [("qk", j) for j in range(4)] + [("a",)] + [("z", j) for j in range(2)]
    u += [("c", t) for t in range(TILES)] + [("v", t) for t in range(TILES)] + [("r", t) for t in range(TILES)]
    u += [("mT", t) for t in range(TILES)] + [("pT", g) for g in range(TILES)] + [("ukT",)]
    u += [("qn", g) for g in range(4)] + [("qr", t) for t in range(TILES)]
    u += [("kd", t) for t in range(TILES)]
    for c in range(len(CHUNKS)):
        u += [("att", c, h) for h in range(GH)]
        u += [x for j in range(2) for x in (("o", c, j), ("u", c, j))]
    u += [("qrT", i) for i in range(5)]
    u += [("ql", h) for h in range(MH)]
    n = len(attention_blocks())
    for i in range(n + 1):
        if i < n:
            u.append(("s", i))
        if i > 0:
            u += [("pt", i - 1), ("ol", i - 1)]
    u += [("ogT", t) for t in range(TILES)] + [("om", g) for g in range(4)]
    u += [("mo", t, c) for t in range(TILES) for c in range(2)]
    for l in range(DEPTH):
        if l:
            u += [("mx", c) for c in range(DK_SLICES)] + [("po", t, c) for t in range(TILES) for c in range(2)]
        u += [("xT", l + 1, i) for i in range(5)]
        u += [("lg", l), ("pos", l)]
        for t in range(TILES):
            u += [("sg", l, t), ("shT", l, t), ("sd", l, t, 0), ("sd", l, t, 1)]
    return u


def attention_blocks():
    out = []
    for h in range(MH):
        out += [([h], 0, 128, 144, "mask0", False), ([h], 128, 128, N_PROMPT, "mask1", False)]
    out.append((list(range(MH)), 2 * P, TAIL, N_PROMPT, "mask_s", False))
    for b in range(2):
        out.append((list(range(4 * b, 4 * b + 4)), SAMPLE0, N_DEC, S_KEYS, "mask_s", True))
    return out


class Steps:

    def __init__(self, eng, sem):
        self.eng, self.sem, self.counts = eng, sem, {}

    def __call__(self, ins, sem=None):
        sem = self.sem if sem is None else sem
        n = self.counts[id(sem)] = self.counts.get(id(sem), 0) + 1
        ins.then_inc(sem, 1)
        self.eng.wait_ge(sem, n)

    def banked(self, ins, banks, name):
        ins.then_inc(banks.empty_sem(name), 1)
        banks.copied(self.eng, name)


def xt_part(i):
    return (i // 2, 4 * (i % 2), 4) if i < 4 else (2, 0, 8)


def bc(ap, axis, n):
    a = ap.unsqueeze(axis)
    shape = list(a.shape)
    shape[axis] = n
    return a.broadcast_to(shape)


def build(nc, a):
    out = a["outs"]
    ctx = ExitStack()
    with ctx:
        mixer_ctx, moe_ctx = ExitStack(), ExitStack()

        def sb(name, shape, dt=F32, scope=ctx):
            return scope.enter_context(nc.sbuf_tensor(f"sb_{name}", shape, dt))

        def sem(name):
            return ctx.enter_context(nc.semaphore(name))

        x = sb("x", [P, TILES, D])
        xt = sb("xt", [P, DK_SLICES, T_PAD])
        cst = sb("cst", [P, CST_W])
        ln_g = sb("ln_g", [P, D])
        ln_b = sb("ln_b", [P, D])
        rbias = sb("rbias", [P, DEPTH, E])
        ln_st = sb("ln_st", [P, TILES, 2, 6])
        ln_mv = sb("ln_mv", [P, TILES, 2])
        ln_rs = sb("ln_rs", [P, TILES])
        eps = sb("eps", [P, 2])

        def const(name):
            return cst[:, slice(*CST[name])]

        def mb(name, shape, dt=F32):
            return sb(name, shape, dt, mixer_ctx)

        w_lo = mb("w_in_lo", [P, 2 * LEVELS * 2 * T_COLS])
        w_hi = mb("w_in_hi", [P, 8 * 1024])
        w_qk = w_lo[:, 0:8 * 512].rearrange("p (k n) -> p k n", k=8)
        w_ac = w_lo[:, 4096:4096 + 8 * 432].rearrange("p (k n) -> p k n", k=8)
        w_v = w_hi[:, 0:4096].rearrange("p (k n) -> p k n", k=8)
        w_r = w_hi[:, 4096:8192].rearrange("p (k n) -> p k n", k=8)
        w_out = w_hi[:, :].rearrange("p (k n) -> p k n", k=8)
        half = LEVELS * 2 * T_COLS
        q_lev = w_lo[:, 0:half].rearrange("p (l j t) -> p l j t", l=LEVELS, j=2)
        k_lev = w_lo[:, half:2 * half].rearrange("p (l j t) -> p l j t", l=LEVELS, j=2)
        q_lat = w_lo[:, 0:8 * T_COLS].rearrange("p (h t) -> p h t", h=8)
        q_rot_t = w_lo[:, 8 * T_COLS:16 * T_COLS].rearrange("p (h t) -> p h t", h=8)
        mix = mb("mix", [P, MIX_W])
        v_sb = mb("v", [P, TILES, 512])
        r_sb = mb("r", [P, TILES, 512])
        r_e = mb("r_e", [P, 512])
        og = mb("og", [P, TILES, 512])
        q_t = mb("q_t", [P, 2, T_COLS])
        k_t = mb("k_t", [P, 2, T_COLS])
        b_t = mb("b_t", [P, 2, T_COLS])
        z_t = mb("z_t", [P, 2, T_COLS])
        u_t = mb("u_t", [P, 2, T_COLS])
        qe_t = mb("qe_t", [P, 2, T_COLS])
        kd_t = mb("kd_t", [P, 2, T_COLS])
        a_t = mb("a_t", [GRANK, T_COLS])
        c_sb = mb("c", [P, TILES, 416])
        sq = mb("sq", [P, 512])
        wg2 = mb("wg2", [GRANK, 256])
        bg = mb("bg", [P, 2])
        g_gla = mb("g_gla", [P, GDV])
        g_q = mb("g_q", [P, QL_R])
        g_kv = mb("g_kv", [P, KVL])
        w_uqn = mb("w_uqn", [P, 2, MH, NOPE])
        w_uqr = mb("w_uqr", [P, 2, MH, ROPE])
        q_few = mb("q_few", [P, MH * (TAIL + N_DEC)])
        q_few_rot = mb("q_few_rot", [ROPE, MH * (TAIL + N_DEC)])
        w_uk = mb("w_uk", [P, 512])
        w_uv = mb("w_uv", [P, MH, MV])
        uk_t = mb("uk_t", [P, 4, 128])
        cq_n = mb("cq_n", [P, TILES, QL_R])
        ckv_n = mb("ckv_n", [P, TILES, KVL])
        kr = mb("kr", [P, TILES, ROPE])
        rot = mb("rot", [P, 2, 128])
        cq_t = mb("cq_t", [P, 2, T_COLS])
        kv_t = mb("kv_t", [P, T_COLS])
        kr_t = mb("kr_t", [ROPE, T_COLS])
        skv_t = mb("skv_t", [P, S_KEYS])
        skr_t = mb("skr_t", [ROPE, S_KEYS])
        past = mb("past", [P, TILES, KVL])
        past_r = mb("past_r", [P, TILES, ROPE])
        q_n_t = mb("q_n_t", [P, 4, T_COLS])
        q_rot = mb("q_rot", [P, TILES, 256])
        msq = mb("msq", [P, 2, 4])
        mrs = mb("mrs", [P, 2, 4])
        att = mb("att", [P, TILES, GH, 64])
        att_m = mb("att_m", [P, (LEVELS + 1) * 64])
        kd = mb("kd", [P, TILES, 256])
        s_p = mb("s_p", [P, 2, 256])
        s_s = mb("s_s", [P, 2, 256])
        gss = mb("gss", [P, TILES * GH])
        grs = mb("grs", [P, TILES * GH])
        sm = z_t
        p_t = q_n_t[:, :, :].rearrange("p g t -> p (g t)")[:, 0:2 * TILES * P].rearrange(
            "p (b k n) -> p b k n", b=2, k=TILES)
        stat = mb("stat", [P, 2, 4])
        mixer_ctx.close()
        o_t = xt

        def eb(name, shape, dt=F32):
            return sb(name, shape, dt, moe_ctx)

        wslot = [eb(f"wslot{u}", [P, 12288]) for u in range(2)]
        w_gate = [w[:, 0:4096].rearrange("p (e n) -> p e n", e=2) for w in wslot]
        w_up = [w[:, 4096:8192].rearrange("p (e n) -> p e n", e=2) for w in wslot]
        w_gu = [w[:, 0:8192].rearrange("p (m e n) -> p m e n", m=2, e=2) for w in wslot]
        w_down = [w[:, 8192:12288].rearrange("p (e n) -> p e n", e=2) for w in wslot]
        sh_gate = wslot[1][:, 0:2048].rearrange("p (k n) -> p k n", k=8)
        sh_up = wslot[1][:, 2048:4096].rearrange("p (k n) -> p k n", k=8)
        sh_down = wslot[1][:, 4096:6144].rearrange("p (k n) -> p k n", k=2)
        pool_w = wslot[1][:, 6144:8192].rearrange("p (g k n) -> p g k n", g=4, k=2)
        pool_s = wslot[1][:, 8192:9216]
        band = wslot[1][:, 9216:9216 + BAND_W]
        acc = eb("acc", [P, TILES, D])
        xh = eb("xh", [P, TILES, D], F32R)
        xl = eb("xl", [P, TILES, D], F32R)
        yh = eb("yh", [P, D], F32R)
        yl = eb("yl", [P, D], F32R)
        xg_own = eb("xg_own", [P, DK_SLICES * 2 * P])
        xgt = [ap.rearrange("p (k n) -> p k n", k=DK_SLICES) for ap in
               (xg_own[:, :], xt[:, :, :].rearrange("p k n -> p (k n)")[:, 0:DK_SLICES * 2 * P])]
        pool_c = xg_own[:, 0:D]
        pick = [eb(f"pick{b}", [P, TILES, 2 * P], F32R) for b in range(2)]
        wpick = eb("wpick", [P, 2, TILES, 4])
        place = [eb(f"place{u}", [P, T_PAD], F32R) for u in range(2)]
        gslot = eb("gslot", [P, 2, 1])
        sg = eb("sg", [P, FE])
        hh = eb("hh", [P, FE])
        ht = eb("ht", [P, 2, P])
        w_rt = eb("w_rt", [P, 8, E])
        sc = eb("sc", [P, TILES, E])
        bi = eb("bi", [P, TILES, E])
        mk = eb("mk", [P, TILES, E])
        mr = eb("mr", [P, TILES, E])
        sel = eb("sel", [P, TILES, E])
        tmp = eb("tmp", [P, TILES, E])
        mx8 = eb("mx8", [P, TILES, 8])
        g_a = eb("g_a", [P, TILES, NG, 4])
        g_b = eb("g_b", [P, TILES, NG, 4])
        g_c = eb("g_c", [P, TILES, NG, 2])
        gs = eb("gs", [P, TILES, NG])
        cmp1 = eb("cmp1", [P, TILES, NG, NG])
        cmp2 = eb("cmp2", [P, TILES, NG, NG])
        rank = eb("rank", [P, TILES, NG])
        wsum = eb("wsum", [P, TILES])
        pos_x = eb("pos_x", [P, TILES, E + 4])
        wt_x = eb("wt_x", [P, TILES, E + 4])
        cnt = eb("cnt", [P, E])
        cmax = eb("cmax", [P, 1])
        thr_c = eb("thr_c", [P, MAX_ROUNDS - 1])
        n_rounds = eb("n_rounds", [P, 1], I32)
        moe_ctx.close()

        def mixc(name):
            return mix[:, slice(*MIX[name])]

        def level_half(ap, v, part):
            b = 2 << v
            n = 4 * CHUNK if b == CHUNK else T_COLS
            h = 1 << v
            return ap[:, 0:n].rearrange("p (m t) -> p m t", t=b)[:, :, part * h:(part + 1) * h]

        banks = Banks(nc, ctx, bank_uses())

        consts_in = sem("consts_in")
        mix_in = sem("mix_in")
        rbias_in = sem("rbias_in")
        y_stored = sem("y_stored")
        x_zeroed = sem("x_zeroed")
        x_in = sem("x_in")
        w_in = [sem(f"w_in{i}") for i in range(4)]
        mixp_in = sem("mixp_in")
        past_in = sem("past_in")
        state_in = sem("state_in")
        w_out_in = sem("w_out_in")
        zeroed = sem("zeroed")
        levels_zeroed = sem("levels_zeroed")
        ln_in = sem("ln_in")
        stored = sem("stored")
        dve_step = sem("dve_step")
        act_step = sem("act_step")
        z_ready = sem("z_ready")
        ls_ready = sem("ls_ready")
        b_ready = sem("b_ready")
        eb_ready = sem("eb_ready")
        dk_ready = sem("dk_ready")
        ek_ready = sem("ek_ready")
        lev_d = sem("lev_d")
        lev_e = sem("lev_e")
        lev_ready = sem("lev_ready")
        qe_ready = sem("qe_ready")
        c_sq = sem("c_sq")
        c_normed = sem("c_normed")
        re_ready = sem("re_ready")
        att_ready = sem("att_ready")
        state_ready = sem("state_ready")
        qrot_ready = sem("qrot_ready")
        skeys_ready = sem("skeys_ready")
        gss_ready = sem("gss_ready")
        grs_ready = sem("grs_ready")
        og_ready = sem("og_ready")
        mx_ready = sem("mx_ready")
        ex_ready = sem("ex_ready")
        p_ready = sem("p_ready")
        x_pre = sem("x_pre")
        var_ready = sem("var_ready")
        rs_ready = sem("rs_ready")
        x_ready = sem("x_ready")
        L = [{n: sem(f"{n}_{l}") for n in (
            "router_in", "shared_in", "gu_in0", "gu_in1", "down_in0", "down_in1", "pool_in", "x_split",
            "lg_exp", "sel_ready", "rounds_ready", "sg_sh", "h_sh", "acc_sh", "init",
            "gu_done0", "gu_done1", "down_done0", "down_done1", "xg_done0", "xg_done1", "xg_copied0", "xg_copied1",
            "pick_ready", "sg_ready", "h_ready", "ht_done", "ht_copied", "place_done", "place_copied",
            "yh_ready0", "yh_ready1", "yl_ready0", "yl_ready1", "sum_done0", "sum_done1", "added0", "added1",
            "y_ready", "next_round")} for l in range(DEPTH)]

        act_gate = [sem(f"act_gate{l}") for l in range(DEPTH)]

        block = ctx.enter_context(nc.Block())

        def load_pair(sp, l, u, pair, parts):
            two = bass.ds(pair * 2, 2) if not isinstance(pair, int) else slice(2 * pair, 2 * pair + 2)
            for name, dst in parts:
                src = a[f"moe_w_{name}"][l][two, :, :]
                src = src.rearrange("e (p k) f -> p e (k f)", p=P)
                sp.dma_start(dst[u], src).then_inc(L[l][f"{'down' if name == 'down' else 'gu'}_in{u}"], 16)

        GU = [("gate", w_gate), ("up", w_up)]
        DN = [("down", w_down)]

        def sp_experts(sp, l):
            s = L[l]
            for name, dst in (("gate", sh_gate), ("up", sh_up), ("down", sh_down)):
                k = dst.shape[1]
                sp.dma_start(dst, a[f"moe_sh_{name}"][l].rearrange("(p k) f -> p k f", k=k)).then_inc(s["shared_in"], 16)
            load_pair(sp, l, 0, 0, GU)
            load_pair(sp, l, 0, 0, DN)
            banks_done = ("sd", l, TILES - 1, 1)
            banks.full(sp, banks_done)
            load_pair(sp, l, 1, 1, GU)
            load_pair(sp, l, 1, 1, DN)
            with sp.Fori(1, GROUPS) as j:
                for u in range(2):
                    sp.wait_ge(s[f"gu_done{u}"], j)
                    load_pair(sp, l, u, 2 * j + u, GU)
                    sp.wait_ge(s[f"down_done{u}"], j)
                    load_pair(sp, l, u, 2 * j + u, DN)
            sp.wait_ge(s["rounds_ready"], 1)
            rounds = sp.value_load(n_rounds[0:1, 0:1], min_val=1, max_val=MAX_ROUNDS)
            with sp.If(rounds - 1):
                with sp.Fori(1, rounds) as r:
                    with sp.Fori(0, GROUPS) as j:
                        for u in range(2):
                            sp.wait_ge(s[f"gu_done{u}"], r * (GROUPS) + j)
                            load_pair(sp, l, u, 2 * j + u, GU)
                            sp.wait_ge(s[f"down_done{u}"], r * (GROUPS) + j)
                            load_pair(sp, l, u, 2 * j + u, DN)

        def xt_in_cols(i):
            t, k0, nk = xt_part(i)
            return xt[:, k0:k0 + nk, t * P:t * P + ROWS[t]]

        @block.sync
        def _(sp):
            sp.dma_start(cst[:, :], a["cst"]).then_inc(consts_in, 16)
            sp.dma_start(x[0:N_META, 0, :], a["meta_tokens"]).then_inc(x_in, 16)
            sp.dma_start(x[N_META:P, 0, :], a["x_prompt"][0, 0:P - N_META, :]).then_inc(x_in, 16)
            sp.dma_start(x[:, 1, :], a["x_prompt"][0, P - N_META:2 * P - N_META, :]).then_inc(x_in, 16)
            sp.wait_ge(x_zeroed, 1)
            sp.dma_start(x[0:TAIL, 2, :], a["x_prompt"][0, 2 * P - N_META:SEQ, :]).then_inc(x_in, 16)
            sp.dma_start(x[SAMPLE_ROW:SAMPLE_ROW + N_DEC, 2, :], a["x_sample"][0]).then_inc(x_in, 16)
            w = a["w_in0"].rearrange("(p k) n -> p k n", k=8)
            for i, (dst, c0, c1) in enumerate(((w_qk, 0, 512), (w_ac, C_A, D_IN), (w_v, C_V, C_R), (w_r, C_R, C_A))):
                sp.dma_start(dst, w[:, :, c0:c1]).then_inc(w_in[i], 16)
            banks.full(sp, ("r", TILES - 1))
            sp.dma_start(w_out, a["w_out0"].rearrange("(k p) n -> p k n", p=P)).then_inc(w_out_in, 16)
            for l in range(DEPTH):
                if l == 0:
                    sp.wait_ge(x_ready, 3)
                    sp.wait_ge(stored, 16 * MIX_STORES)
                else:
                    sp.wait_ge(x_ready, 6)
                    s = L[l]
                    sp.dma_start(pool_w, a["pool_w"].rearrange("g (k p) n -> p g k n", p=P)).then_inc(s["pool_in"], 16)
                    sp.dma_start(pool_s, a["pool_scale"].partition_broadcast(P)).then_inc(s["pool_in"], 16)
                    sp.dma_start(band, a["band"]).then_inc(s["pool_in"], 16)
                    sp.wait_ge(s["init"], 1)
                    sp.dma_start(pool_c[0:15, :], a["cache_pool"][0]).then_inc(s["pool_in"], 16)
                sp.dma_start(w_rt[:, :, :], a["moe_router_w"][l].rearrange("(p k) e -> p k e", k=8)).then_inc(L[l]["router_in"], 16)
                if l == 1:
                    banks.full(sp, ("po", TILES - 1, 1))
                    banks.copied(sp, ("po", TILES - 1, 1))
                sp_experts(sp, l)
            sp.wait_ge(x_ready, 12)
            sp.dma_start(out["y_prompt"][0, 0:P - N_META, :], x[N_META:P, 0, :]).then_inc(y_stored, 16)
            sp.dma_start(out["y_prompt"][0, P - N_META:2 * P - N_META, :], x[:, 1, :]).then_inc(y_stored, 16)
            sp.dma_start(out["y_prompt"][0, 2 * P - N_META:SEQ, :], x[0:TAIL, 2, :]).then_inc(y_stored, 16)
            sp.dma_start(out["y_sample"][0], x[SAMPLE_ROW:SAMPLE_ROW + N_DEC, 2, :]).then_inc(y_stored, 16)
            sp.wait_ge(y_stored, 16 * 4)
            sp.wait_ge(stored, 16 * (MIX_STORES + 2))

        @block.gpsimd
        def _(gp):
            gp.memset(x[:, 2, :], 0.0).then_inc(x_zeroed, 1)
            gp.dma_start(bg[:, :], a["gla_b_g"].rearrange("(j p) -> p j", p=P), allow_slow_non_contiguous=True).then_inc(mixp_in, 16)
            gp.dma_start(wg2[:, :], a["gla_w_g2"]).then_inc(mixp_in, 16)
            gp.dma_start(mix[:, :], a["mix"]).then_inc(mix_in, 16)
            gp.dma_start(g_q[:, :], a["mla_q_norm_g"].partition_broadcast(P)).then_inc(mixp_in, 16)
            gp.dma_start(g_kv[:, :], a["mla_kv_norm_g"].partition_broadcast(P)).then_inc(mixp_in, 16)
            gp.dma_start(g_gla[:, :], a["gla_norm_g"].partition_broadcast(P)).then_inc(mixp_in, 16)
            for k in range(2):
                uq = a["mla_w_uq"][k * P:(k + 1) * P, :].rearrange("p (h n) -> p h n", h=MH)
                gp.dma_start(w_uqn[:, k, :, :], uq[:, :, 0:NOPE]).then_inc(mixp_in, 16)
                gp.dma_start(w_uqr[:, k, :, :], uq[:, :, NOPE:]).then_inc(mixp_in, 16)
            gp.dma_start(w_uk[:, :], a["mla_w_uk"].rearrange("c h n -> c (h n)")).then_inc(mixp_in, 16)
            gp.dma_start(w_uv[:, :, :], a["mla_w_uv"]).then_inc(mixp_in, 16)
            for l in range(DEPTH):
                gp.dma_start(rbias[:, l, :], a["moe_router_b"][l].partition_broadcast(P)).then_inc(rbias_in, 16)
            ck, ckr = a["cache_mla_ckv"][0], a["cache_mla_krope"][0]
            for src, dst in ((ck, past), (ckr, past_r)):
                gp.memset(dst[:, 2, :], 0.0).then_inc(zeroed, 1)
            gp.wait_ge(zeroed, 2)
            for src, dst in ((ck, past), (ckr, past_r)):
                gp.dma_start(dst[:, 0:2, :], src[0:2 * P, :].rearrange("(t p) c -> p t c", p=P)).then_inc(past_in, 16)
                gp.dma_start(dst[0:TAIL, 2, :], src[2 * P:N_KEYS_PAST, :]).then_inc(past_in, 16)
            for t in (og[:, 2, :], kd_t[:, :, :], s_p[:, :, :], s_s[:, :, :], skv_t[:, :], skr_t[:, :],
                      qe_t[:, :, :], eps[:, 0:1]):
                gp.memset(t, LN_EPS if t.shape[-1] == 1 else 0.0).then_inc(zeroed, 1)
            gp.memset(eps[:, 1:2], RMS_EPS).then_inc(zeroed, 1)
            gp.memset(msq[:, :, :], 1.0).then_inc(zeroed, 1)
            gp.memset(gss[:, :], 1.0).then_inc(zeroed, 1)
            gp.wait_ge(zeroed, ZEROED)
            for h in range(GH):
                j, b = divmod(h, 2)
                gp.dma_start(s_s[64 * b:64 * b + 64, j, 128 * b:128 * b + 128], a["state_gla"][0, h]).then_inc(state_in, 16)
            banks.full(gp, ("c", TILES - 1))
            gp.memset(w_lo[:, :], 0.0).then_inc(levels_zeroed, 1)

            def load_ln(l, i):
                gp.dma_start(ln_g[:, :], a["ln_g"][l, i].partition_broadcast(P)).then_inc(ln_in, 16)
                gp.dma_start(ln_b[:, :], a["ln_b"][l, i].partition_broadcast(P)).then_inc(ln_in, 16)

            load_ln(0, 0)
            gp.wait_ge(c_normed, 3)
            for name, src in (("ckv", ckv_n), ("krope", kr)):
                po, so = out[f"prompt_{name}"][0], out[f"sample_{name}"][0]
                gp.dma_start(po[0:2 * P, :].rearrange("(t p) c -> p t c", p=P), src[:, 0:2, :]).then_inc(stored, 16)
                gp.dma_start(po[2 * P:N_PROMPT, :], src[0:TAIL, 2, :]).then_inc(stored, 16)
                gp.dma_start(so, src[SAMPLE_ROW:SAMPLE_ROW + N_DEC, 2, :]).then_inc(stored, 16)
            for j in range(2):
                banks.copied(gp, ("u", 4, j))
                banks.copied(gp, ("u", 5, j))
            for st, o in ((s_p, out["prompt_gla_state"]), (s_s, out["sample_gla_state"])):
                for h in range(GH):
                    j, b = divmod(h, 2)
                    gp.dma_start(o[0, h], st[64 * b:64 * b + 64, j, 128 * b:128 * b + 128]).then_inc(stored, 16)
            for l in range(DEPTH):
                s = L[l]
                if l:
                    gp.wait_ge(x_ready, 6)
                    gp.dma_start(out["prompt_pool_rows"][0], x[TAIL - 15:TAIL, 2, :]).then_inc(stored, 16)
                    e = SAMPLE_ROW + N_DEC
                    gp.dma_start(out["sample_pool_rows"][0], x[e - 15:e, 2, :]).then_inc(stored, 16)
                    gp.memset(pool_c, 0.0).then_inc(s["init"], 1)
                    load_ln(1, 0)
                gp.wait_ge(x_ready, 3 + 6 * l)
                if l == 0:
                    gp.wait_ge(stored, 16 * MIX_STORES)
                for t in (place[1][:, :], place[0][:, T_COLS:], yh[:, :], yl[:, :], xh[:, 2, :], xl[:, 2, :]):
                    gp.memset(t.bitcast(F32), 0.0).then_inc(s["init"], 1)
                gp.memset(xt[:, :, T_COLS:], 0.0).then_inc(s["init"], 1)
                load_ln(l, 1)

        ident = const("ident")

        def transpose(pe, dst, src):
            n = src.shape[0]
            return pe.transpose(dst, src, ident[0:n, 0:n])

        def pe_transpose_x(pe, n):
            for i in range(5):
                t, k0, nk = xt_part(i)
                rows = ROWS[t]
                if n or i == 0:
                    pass
                ps = banks.open(pe, ("xT", n, i))
                for k in range(nk):
                    last = transpose(pe, ps[:, k * rows:(k + 1) * rows], x[0:rows, t, k0 + k::8])
                last.then_inc(banks.fill_sem(("xT", n, i)), 1)

        def accumulate(pe, dst, pairs):
            for i, (lhs, rhs) in enumerate(pairs):
                last = pe.matmul(dst, lhs, rhs, start=i == 0, stop=i == len(pairs) - 1)
            return last

        def pe_experts(pe, l):
            s = L[l]
            gu_b, ht_b = banks.tile[0], banks.tile[1]
            xg_b, y_b, cb_b = banks.tile[2:4], banks.tile[4:6], banks.tile[6:8]
            banks.all_copied(pe, ("sd", l, TILES - 1, 1))

            def gather(b, u):
                for kk in range(4):
                    for i, part in enumerate((xh, xl)):
                        for t in range(TILES):
                            last = pe.matmul(xg_b[kk // 2][:, (kk % 2) * 2 * P:(kk % 2 + 1) * 2 * P], part[:, t, 4 * u + kk::8],
                                             pick[b][:, t, :], start=i == 0 and t == 0, stop=i == 1 and t == 2)
                    if kk % 2:
                        last.then_inc(s[f"xg_done{kk // 2}"], 1)

            def place_add(u, n, t):
                for c in range(2):
                    pe.wait_ge(s[f"added{c}"], n + t + 1)
                    for i, part in enumerate((yh, yl)):
                        last = pe.matmul(cb_b[c][:, :], place[u][:, t * P:(t + 1) * P],
                                         part[:, c * 512:(c + 1) * 512], start=i == 0, stop=i == 1)
                    last.then_inc(s[f"sum_done{c}"], 1)

            def down(u, c, k):
                for e in range(2):
                    last = pe.matmul(y_b[c][64 * e:64 * e + 64, :], ht[:, k, 64 * e:64 * e + 64],
                                     w_down[u][:, e, k * D + c * 512:k * D + (c + 1) * 512],
                                     start=k == 0, stop=k == 1)
                return last

            pe.wait_ge(s["rounds_ready"], 1)
            rounds = pe.value_load(n_rounds[0:1, 0:1], min_val=1, max_val=MAX_ROUNDS)
            pe.wait_ge(s["x_split"], 2)
            pe.wait_ge(s["init"], 7 + l)
            pe.wait_ge(s["pick_ready"], 1)
            for u in range(2):
                if u:
                    pe.wait_ge(s["xg_copied0"], 1)
                    pe.wait_ge(s["xg_copied1"], 1)
                gather(0, u)
            with pe.Fori(0, rounds) as r:
                with pe.Fori(0, GROUPS // 2) as j:
                    for b in range(2):
                        for u in range(2):
                            n = r * GROUPS + 2 * j + b
                            i = 2 * n + u
                            pe.wait_ge(s[f"gu_in{u}"], 32 * n + 32)
                            if u == 0:
                                pe.wait_ge(s["xg_copied0"], i + 2)
                                pe.wait_ge(s["xg_copied1"], i + 2)
                            pe.wait_ge(s["place_copied"], i + 1)
                            for k in range(DK_SLICES):
                                for e in range(2):
                                    sl = slice(u * P + 64 * e, u * P + 64 * e + 64)
                                    last = pe.matmul(gu_b[64 * e:64 * e + 64, :], xgt[b][:, k, sl],
                                                     w_gu[u][:, :, e, k * FE:(k + 1) * FE],
                                                     start=k == 0, stop=k == DK_SLICES - 1)
                            last.then_inc(s[f"gu_done{u}"], 1)
                            if u == 0:
                                pe.wait_ge(s["pick_ready"], n + 2)
                            else:
                                pe.wait_ge(s["xg_copied0"], i + 2)
                                pe.wait_ge(s["xg_copied1"], i + 2)
                            gather(1 - b, u)
                            pe.wait_ge(s["h_ready"], i + 2)
                            for k in range(2):
                                last = transpose(pe, ht_b[:, k * P:(k + 1) * P], hh[:, k::2])
                            last.then_inc(s["ht_done"], 1)
                            pu = slice(u * P, (u + 1) * P)
                            for t in range(TILES):
                                rows = ROWS[t]
                                transpose(pe, gu_b[:, t * P:t * P + rows], pick[b][0:rows, t, pu].bitcast(F32))
                            accumulate(pe, gu_b[:, T_COLS:T_COLS + 2], [
                                (pick[b][:, t, pu].bitcast(F32), wpick[:, b, t, 2 * u:2 * u + 2])
                                for t in range(TILES)]).then_inc(s["place_done"], 1)
                            pe.wait_ge(s["y_ready"], 2 * i + 1)
                            place_add(1 - u, 3 * i, 0)
                            pe.wait_ge(s["ht_copied"], i + 1)
                            pe.wait_ge(s[f"down_in{u}"], 16 * n + 16)
                            down(u, 0, 0)
                            down(u, 0, 1)
                            place_add(1 - u, 3 * i, 1)
                            down(u, 1, 0)
                            place_add(1 - u, 3 * i, 2)
                            down(u, 1, 1).then_inc(s[f"down_done{u}"], 1)
            total = rounds * PAIRS
            pe.wait_ge(s["y_ready"], 2 * total + 1)
            for t in range(TILES):
                place_add(1, 3 * total, t)

        @block.tensor
        def _(pe):
            for l in range(DEPTH):
                for n in ("added0", "added1", "place_copied", "y_ready", "h_ready", "place_done"):
                    pe.sem_inc(L[l][n], 1)
            pe.wait_ge(consts_in, 16)
            pe.wait_ge(x_in, 16 * 5)
            pe_transpose_x(pe, 0)

            def stage(name, pairs_of):
                ps = banks.open(pe, name)
                return pairs_of(ps).then_inc(banks.fill_sem(name), 1)

            for i in range(5):
                banks.copied(pe, ("xT", 0, i))
            pe.wait_ge(w_in[0], 16)
            for j in range(4):
                stage(("qk", j), lambda ps: accumulate(pe, ps[:, 0:T_COLS], [
                    (w_qk[:, k, j * P:(j + 1) * P], xt[:, k, 0:T_COLS]) for k in range(8)]))
            pe.wait_ge(w_in[1], 16)
            stage(("a",), lambda ps: accumulate(pe, ps[0:GRANK, 0:T_COLS], [
                (w_ac[:, k, 0:GRANK], xt[:, k, 0:T_COLS]) for k in range(8)]))
            banks.copied(pe, ("a",))
            pe.wait_ge(mixp_in, 16 * MIX_PARAMS)
            for j in range(2):
                stage(("z", j), lambda ps: pe.matmul(ps[:, 0:T_COLS], wg2[:, j * P:(j + 1) * P], a_t[:, :],
                                                     start=True, stop=True))
            for name, w, c0, n in (("c", w_ac, GRANK, 416), ("v", w_v, 0, 512), ("r", w_r, 0, 512)):
                if name != "c":
                    pe.wait_ge(w_in[2 if name == "v" else 3], 16)
                for t in range(TILES):
                    rows = ROWS[t]
                    stage((name, t), lambda ps: accumulate(pe, ps[0:rows, 0:n], [
                        (xt[:, k, t * P:t * P + rows], w[:, k, c0:c0 + n]) for k in range(8)]))
            for t in range(TILES):
                rows = ROWS[t]
                pe.wait_ge(c_normed, t + 1)
                ps = banks.open(pe, ("mT", t))
                for k in range(2):
                    transpose(pe, ps[:, k * P:k * P + rows], cq_n[0:rows, t, k * P:(k + 1) * P])
                transpose(pe, ps[:, 256:256 + rows], ckv_n[0:rows, t, :])
                transpose(pe, ps[0:ROPE, 384:384 + rows], kr[0:rows, t, :]).then_inc(banks.fill_sem(("mT", t)), 1)
            pe.wait_ge(past_in, 16 * 4)
            for g in range(TILES):
                rows = P if g < 2 else TAIL
                ps = banks.open(pe, ("pT", g))
                transpose(pe, ps[:, 0:rows], past[0:rows, g, :])
                transpose(pe, ps[0:ROPE, P:P + rows], past_r[0:rows, g, :]).then_inc(banks.fill_sem(("pT", g)), 1)
            ps = banks.open(pe, ("ukT",))
            for g in range(4):
                last = transpose(pe, ps[:, g * P:(g + 1) * P], w_uk[:, g * P:(g + 1) * P])
            last.then_inc(banks.fill_sem(("ukT",)), 1)
            for t in range(TILES):
                banks.copied(pe, ("mT", t))
            for g in range(4):
                stage(("qn", g), lambda ps: accumulate(pe, ps[:, 0:T_COLS], [
                    (w_uqn[:, k, 2 * g:2 * g + 2, :].rearrange("p h n -> p (h n)"), cq_t[:, k, :]) for k in range(2)]))
            for t in range(TILES):
                rows = ROWS[t]
                stage(("qr", t), lambda ps: accumulate(pe, ps[0:rows, 0:256], [
                    (cq_t[:, k, t * P:t * P + rows], w_uqr[:, k, :, :].rearrange("p h n -> p (h n)")) for k in range(2)]))
            pe.wait_ge(qe_ready, 2)
            for t in range(TILES):
                rows = ROWS[t]
                ps = banks.open(pe, ("kd", t))
                for j in range(2):
                    last = transpose(pe, ps[0:rows, j * P:(j + 1) * P], kd_t[:, j, t * P:t * P + rows])
                last.then_inc(banks.fill_sem(("kd", t)), 1)
            pe.wait_ge(lev_ready, LEVELS)
            pe.wait_ge(zeroed, ZEROED)
            pe.wait_ge(state_in, 16 * GH)
            for t in range(TILES):
                banks.copied(pe, ("kd", t))
            for c, (t, pb, n) in enumerate(CHUNKS):
                c0 = t * P + pb
                levels = int(math.log2(n))
                w = 32 if n == 32 else 64
                for h in range(GH):
                    j, hb = h // 2, 64 * (h % 2)
                    ps = banks.open(pe, ("att", c, h))
                    for v in range(levels + 1):
                        kk = k_t[hb:hb + 64, j, c0:c0 + n] if v == 0 else k_lev[hb:hb + 64, v - 1, j, c0:c0 + n]
                        qq = q_t[hb:hb + 64, j, c0:c0 + n] if v == 0 else q_lev[hb:hb + 64, v - 1, j, c0:c0 + n]
                        last = pe.matmul(ps[pb:pb + n, v * w:v * w + n], kk, qq, start=True, stop=True)
                    last.then_inc(banks.fill_sem(("att", c, h)), 1)
                st = s_s if c == 5 else s_p
                if 0 < c < 5:
                    for j in range(2):
                        banks.copied(pe, ("u", c - 1, j))
                for j in range(2):
                    ps = banks.open(pe, ("o", c, j))
                    pe.matmul(ps[pb:pb + n, 0:256], qe_t[:, j, c0:c0 + n], st[:, j, :], start=True, stop=False)
                    for b in range(2):
                        h = 2 * j + b
                        pe.wait_ge(att_ready, 4 * c + h + 1)
                        last = pe.matmul(ps[pb:pb + n, b * P:(b + 1) * P], att[pb:pb + n, t, h, 0:n],
                                         v_sb[pb:pb + n, t, h * P:(h + 1) * P], start=False, stop=b == 1)
                    last.then_inc(banks.fill_sem(("o", c, j)), 1)
                    stage(("u", c, j), lambda ps: pe.matmul(ps[:, 0:256], kd[pb:pb + n, t, j * P:(j + 1) * P],
                                                            v_sb[pb:pb + n, t, j * 256:(j + 1) * 256],
                                                            start=True, stop=True))
            pe.wait_ge(qrot_ready, TILES)
            for i in range(5):
                t, h0, nh = xt_part(i)
                rows = ROWS[t]
                ps = banks.open(pe, ("qrT", i))
                for h in range(nh):
                    last = transpose(pe, ps[0:ROPE, h * rows:(h + 1) * rows], q_rot[0:rows, t, (h0 + h) * ROPE:(h0 + h + 1) * ROPE])
                last.then_inc(banks.fill_sem(("qrT", i)), 1)
            for h in range(MH):
                g, hb = h // 2, 64 * (h % 2)
                stage(("ql", h), lambda ps: pe.matmul(ps[:, 0:T_COLS], uk_t[hb:hb + 64, g, :], q_n_t[hb:hb + 64, g, :],
                                                      start=True, stop=True))
            blocks = attention_blocks()
            for h in range(MH):
                banks.copied(pe, ("ql", h))
            for i in range(5):
                banks.copied(pe, ("qrT", i))
            pe.wait_ge(skeys_ready, 2)
            for i in range(len(blocks) + 1):
                if i < len(blocks):
                    hs, q0, nq, nk, _, sample = blocks[i]
                    kt, krt = (skv_t, skr_t) if sample else (kv_t, kr_t)
                    if len(hs) == 1:
                        ql, qr = q_lat[:, hs[0], q0:q0 + nq], q_rot_t[0:ROPE, hs[0], q0:q0 + nq]
                    else:
                        c0 = MH * TAIL + hs[0] * N_DEC if sample else 0
                        ql, qr = q_few[:, c0:c0 + P], q_few_rot[:, c0:c0 + P]
                    stage(("s", i), lambda ps: accumulate(pe, ps[:, 0:nk], [
                        (ql, kt[:, 0:nk]),
                        (qr, krt[:, 0:nk])]))
                if i > 0:
                    m = i - 1
                    hs, q0, nq, nk, _, sample = blocks[m]
                    keys = [(k, min(P, nk - k * P)) for k in range(-(-nk // P))]
                    pe.wait_ge(p_ready, m + 1)
                    ps = banks.open(pe, ("pt", m))
                    for k, rows in keys:
                        last = transpose(pe, ps[0:rows, k * P:(k + 1) * P], sm[:, m % 2, k * P:k * P + rows])
                    last.then_inc(banks.fill_sem(("pt", m)), 1)
                    banks.copied(pe, ("pt", m))
                    src = past if sample else ckv_n
                    stage(("ol", m), lambda ps: accumulate(pe, ps[:, 0:P], [
                        (src[0:rows, k, :], p_t[0:rows, m % 2, k, :]) for k, rows in keys]))
            pe.wait_ge(og_ready, TILES)
            for t in range(TILES):
                rows = ROWS[t]
                ps = banks.open(pe, ("ogT", t))
                for h in range(GH):
                    last = transpose(pe, ps[:, h * rows:(h + 1) * rows], og[0:rows, t, h * P:(h + 1) * P])
                last.then_inc(banks.fill_sem(("ogT", t)), 1)
            for m in range(len(blocks)):
                banks.copied(pe, ("ol", m))
            for g in range(4):
                ps = banks.open(pe, ("om", g))
                for b in range(2):
                    last = pe.matmul(ps[64 * b:64 * b + 64, 0:T_COLS], w_uv[:, 2 * g + b, :], q_lat[:, 2 * g + b, :],
                                     start=True, stop=True)
                last.then_inc(banks.fill_sem(("om", g)), 1)
            for t in range(TILES):
                banks.copied(pe, ("ogT", t))
            for g in range(4):
                banks.copied(pe, ("om", g))
            pe.wait_ge(w_out_in, 16)
            for t in range(TILES):
                rows = ROWS[t]
                for c in range(2):
                    stage(("mo", t, c), lambda ps: accumulate(pe, ps[0:rows, :], [
                        (o_t[:, k, t * P:t * P + rows], w_out[:, k, c * 512:(c + 1) * 512]) for k in range(8)]))
            for l in range(DEPTH):
                s = L[l]
                if l:
                    pe.wait_ge(x_ready, 6)
                    pe.wait_ge(s["pool_in"], 16 * 4)
                    bd = {n: band[:, slice(*BAND[n])].rearrange("p (g t) -> p g t", g=4) for n in BAND}
                    for c in range(DK_SLICES):
                        g, cc = c // 2, slice(c * P, (c + 1) * P)
                        ps = banks.open(pe, ("mx", c))
                        pe.matmul(ps[:, 0:128], x[:, 0, cc], bd["own0"][:, g, :], start=True, stop=True)
                        accumulate(pe, ps[:, 128:256], [(x[:, 0, cc], bd["prev1"][:, g, :]), (x[:, 1, cc], bd["own1"][:, g, :])])
                        accumulate(pe, ps[:, 256:320], [(x[:, 1, cc], bd["prev2"][:, g, :]), (x[0:64, 2, cc], bd["own2"][0:64, g, :]),
                                                        (pool_c[0:64, cc], bd["cache"][0:64, g, :])]).then_inc(banks.fill_sem(("mx", c)), 1)
                    for c in range(DK_SLICES):
                        banks.copied(pe, ("mx", c))
                    for t in range(TILES):
                        rows = ROWS[t]
                        for c in range(2):
                            ps = banks.open(pe, ("po", t, c))
                            for g in range(2):
                                last = accumulate(pe, ps[0:rows, g * PG:(g + 1) * PG], [
                                    (xt[:, 4 * c + 2 * g + k, t * P:t * P + rows], pool_w[:, 2 * c + g, k, :]) for k in range(2)])
                            last.then_inc(banks.fill_sem(("po", t, c)), 1)
                pe.wait_ge(x_ready, 3 + 6 * l)
                pe_transpose_x(pe, l + 1)
                for i in range(5):
                    banks.copied(pe, ("xT", l + 1, i))
                pe.wait_ge(s["init"], 7 + l)
                pe.wait_ge(s["router_in"], 16)
                ps = banks.open(pe, ("lg", l))
                for t in range(TILES):
                    last = accumulate(pe, ps[:, t * E:(t + 1) * E], [(xt[:, k, t * P:(t + 1) * P], w_rt[:, k, :]) for k in range(8)])
                last.then_inc(banks.fill_sem(("lg", l)), 1)
                pe.wait_ge(s["sel_ready"], 1)
                ps = banks.open(pe, ("pos", l))
                for t in range(TILES):
                    accumulate(pe, ps[:, t * E:(t + 1) * E], [(const("ones"), sel[:, i, :]) for i in range(t)] +
                               [(const("before"), sel[:, t, :])])
                accumulate(pe, ps[:, TILES * E:(TILES + 1) * E], [(const("ones"), sel[:, i, :]) for i in range(TILES)])\
                    .then_inc(banks.fill_sem(("pos", l)), 1)
                pe.wait_ge(s["shared_in"], 16 * 3)
                for t in range(TILES):
                    rows = ROWS[t]
                    tc = slice(t * P, t * P + rows)
                    ps = banks.open(pe, ("sg", l, t))
                    accumulate(pe, ps[0:rows, 0:FE], [(xt[:, k, tc], sh_gate[:, k, :]) for k in range(8)])
                    accumulate(pe, ps[0:rows, FE:2 * FE], [(xt[:, k, tc], sh_up[:, k, :]) for k in range(8)])\
                        .then_inc(banks.fill_sem(("sg", l, t)), 1)
                    banks.copied(pe, ("sg", l, t))
                    ps = banks.open(pe, ("shT", l, t))
                    for k in range(2):
                        last = transpose(pe, ps[:, k * P:k * P + rows], hh[0:rows, k::2])
                    last.then_inc(banks.fill_sem(("shT", l, t)), 1)
                    banks.copied(pe, ("shT", l, t))
                    for c in range(2):
                        stage(("sd", l, t, c), lambda ps: accumulate(pe, ps[0:rows, :], [
                            (ht[:, k, 0:rows], sh_down[:, k, c * 512:(c + 1) * 512]) for k in range(2)]))
                pe_experts(pe, l)

        def act_experts(act, l):
            s = L[l]
            gu_b, ht_b = banks.tile[0], banks.tile[1]
            act.wait_ge(s["rounds_ready"], 1)
            rounds = act.value_load(n_rounds[0:1, 0:1], min_val=1, max_val=MAX_ROUNDS)

            def copy_xg(b, u, n):
                act.wait_ge(s["xg_done0"], n)
                act.activation(xgt[b][:, 4 * u:4 * u + 2, :], banks.tile[2][:, :].rearrange("p (k n) -> p k n", k=2), ACT.Copy)\
                   .then_inc(s["xg_copied0"], 1)

            for u in range(2):
                copy_xg(0, u, u + 1)
            with act.Fori(0, rounds) as r:
                with act.Fori(0, GROUPS // 2) as j:
                    for b in range(2):
                        for u in range(2):
                            n = r * GROUPS + 2 * j + b
                            i = 2 * n + u
                            act.wait_ge(s[f"gu_done{u}"], n + 1)
                            act.wait_ge(s["h_ready"], i + 1)
                            act.activation(sg[:, :], gu_b[:, 0:FE], ACT.Silu).then_inc(s["sg_ready"], 1)
                            copy_xg(1 - b, u, i + 3)
                            act.wait_ge(s["ht_done"], i + 1)
                            act.activation(ht[:, :, :], ht_b[:, 0:2 * P].rearrange("p (k n) -> p k n", k=2), ACT.Copy)\
                               .then_inc(s["ht_copied"], 1)
                            act.wait_ge(s["place_done"], i + 2)
                            for e in range(2):
                                act.activation(gslot[64 * e:64 * e + 64, u, :],
                                               gu_b[64 * e:64 * e + 64, T_COLS + e:T_COLS + e + 1], ACT.Copy)\
                                   .then_inc(act_gate[l], 1)
                            act.activation(place[u][:, 0:T_COLS], gu_b[:, 0:T_COLS], ACT.Copy).then_inc(s["place_copied"], 1)
                            act.wait_ge(s[f"down_done{u}"], n + 1)
                            act.wait_ge(act_gate[l], 2 * i + 2)
                            for c in range(2):
                                act.activation(yh[:, c * 512:(c + 1) * 512], banks.tile[4 + c][:, :], ACT.Copy,
                                               scale=gslot[:, u, :]).then_inc(s[f"yh_ready{c}"], 1)

        @block.scalar
        def _(act):
            step = Steps(act, act_step)

            def copy(dst, name, src=None):
                ps = banks.full(act, name)
                act.activation(dst, src(ps) if src else ps, ACT.Copy).then_inc(banks.empty_sem(name), 1)

            def copy_xt(n):
                for i in range(0, 5, 2):
                    t, k0, nk = xt_part(i)
                    copy(xt_in_cols(i), ("xT", n, i), lambda ps: ps[:, 0:nk * ROWS[t]].rearrange("p (k n) -> p k n", k=nk))

            def rsqrt(dst, src, scale, bias, sem=None):
                step(act.activation(dst, src, ACT.Ln, scale=scale, bias=bias))
                step(act.activation(dst, dst, ACT.Exp, scale=-0.5), sem)

            def ln_rsqrt(n):
                for t in range(TILES):
                    rows = ROWS[t]
                    act.wait_ge(var_ready, 3 * n + t + 1)
                    rsqrt(ln_rs[0:rows, t:t + 1], ln_mv[0:rows, t, 1:2], 1.0, eps[0:rows, 0:1], rs_ready)

            copy_xt(0)
            for j in range(2, 4):
                copy(k_t[:, j - 2, :], ("qk", j), lambda ps: ps[:, 0:T_COLS])
            copy(a_t[:, :], ("a",), lambda ps: ps[0:GRANK, 0:T_COLS])
            act.wait_ge(z_ready, 2)
            step(act.activation(u_t[:, :, :], z_t[:, :, :], ACT.Abs))
            step(act.activation(u_t[:, :, :], u_t[:, :, :], ACT.Exp, scale=-1.0))
            step(act.activation(u_t[:, :, :], u_t[:, :, :], ACT.Ln, bias=1.0), ls_ready)
            act.wait_ge(zeroed, ZEROED)
            for t in range(TILES):
                rows = ROWS[t]
                banks.copied(act, ("c", t))
                step(act.activation(sq[0:rows, 0:QL_R], c_sb[0:rows, t, 0:QL_R], ACT.Square, accum_out=msq[0:rows, 0, t:t + 1]))
                step(act.activation(sq[0:rows, 0:KVL], c_sb[0:rows, t, QL_R:QL_R + KVL], ACT.Square, accum_out=msq[0:rows, 1, t:t + 1]))
            rsqrt(mrs[:, 0, 0:3], msq[:, 0, 0:3], 1.0 / QL_R, eps[:, 1:2], c_sq)
            rsqrt(mrs[:, 1, 0:3], msq[:, 1, 0:3], 1.0 / KVL, eps[:, 1:2], c_sq)
            act.wait_ge(b_ready, 1)
            step(act.activation(u_t[:, :, :], b_t[:, :, :], ACT.Exp), eb_ready)
            act.wait_ge(dk_ready, 1)
            step(act.activation(kd_t[:, :, :], kd_t[:, :, :], ACT.Exp), ek_ready)
            for t in range(TILES):
                copy(v_sb[0:ROWS[t], t, :], ("v", t), lambda ps: ps[0:ROWS[t], :])
            for v in range(LEVELS):
                act.wait_ge(lev_d, v + 1)
                for w, part in ((q_lev, 1), (k_lev, 0)):
                    for j in range(2):
                        ap = level_half(w[:, v, j, :], v, part)
                        ins = act.activation(ap, ap, ACT.Exp)
                        if part == 0 and j == 1:
                            step(ins, lev_e)
            for t in range(TILES):
                rows = ROWS[t]
                ps = banks.full(act, ("r", t))
                if t:
                    banks.copied(act, ("r", t - 1))
                step(act.activation(r_e[0:rows, :], ps[0:rows, :], ACT.Exp, scale=-1.0), re_ready)
            for t in range(TILES):
                rows, n = ROWS[t], ("mT", t)
                cols = slice(t * P, t * P + rows)
                ps = banks.full(act, n)
                act.activation(cq_t[:, :, cols], ps[:, 0:256].rearrange("p (k n) -> p k n", k=2)[:, :, 0:rows], ACT.Copy)
                act.activation(kv_t[:, cols], ps[:, 256:256 + rows], ACT.Copy)
                act.activation(kr_t[:, cols], ps[0:ROPE, 384:384 + rows], ACT.Copy).then_inc(banks.empty_sem(n), 1)
            for g in range(TILES):
                rows, n = P if g < 2 else TAIL, ("pT", g)
                ps = banks.full(act, n)
                act.activation(skv_t[:, g * P:g * P + rows], ps[:, 0:rows], ACT.Copy)
                act.activation(skr_t[:, g * P:g * P + rows], ps[0:ROPE, P:P + rows], ACT.Copy).then_inc(banks.empty_sem(n), 1)
            copy(uk_t[:, :, :], ("ukT",), lambda ps: ps[:, :].rearrange("p (g n) -> p g n", g=4))
            for g in range(4):
                copy(q_n_t[:, g, :], ("qn", g), lambda ps: ps[:, 0:T_COLS])
            for t in range(TILES):
                rows = ROWS[t]
                copy(kd[0:rows, t, :], ("kd", t), lambda ps: ps[0:rows, 0:256])
            banks.copied(act, ("mT", 2))
            own = slice(SAMPLE_ROW, SAMPLE_ROW + N_DEC)
            act.wait_ge(past_in, 16 * 4)
            act.wait_ge(c_normed, 3)
            act.activation(skv_t[:, SAMPLE0:], kv_t[:, SAMPLE0:], ACT.Copy)
            act.activation(skr_t[:, SAMPLE0:], kr_t[:, SAMPLE0:], ACT.Copy)
            act.activation(past[own, 2, :], ckv_n[own, 2, :], ACT.Copy).then_inc(skeys_ready, 1)
            for i in range(5):
                t, h0, nh = xt_part(i)
                rows = ROWS[t]
                copy(q_rot_t[0:ROPE, h0:h0 + nh, t * P:t * P + rows], ("qrT", i),
                     lambda ps: ps[0:ROPE, 0:nh * rows].rearrange("p (h n) -> p h n", h=nh))
            for h in range(MH):
                copy(q_lat[:, h, :], ("ql", h), lambda ps: ps[:, 0:T_COLS])
            for h in range(MH):
                banks.copied(act, ("ql", h))
            for i in range(5):
                banks.copied(act, ("qrT", i))
            for src, dst in ((q_lat, q_few), (q_rot_t[0:ROPE, :, :], q_few_rot)):
                for c0, q0, nq in ((0, 2 * P, TAIL), (MH * TAIL, SAMPLE0, N_DEC)):
                    ins = act.activation(dst[:, c0:c0 + MH * nq].rearrange("p (h t) -> p h t", h=MH), src[:, :, q0:q0 + nq], ACT.Copy)
            ins.then_inc(skeys_ready, 1)
            act.wait_ge(gss_ready, TILES)
            rsqrt(grs[:, :], gss[:, :], 1.0 / GDV, eps[:, 1:2], grs_ready)
            blocks = attention_blocks()

            def exp_block(m):
                nk = blocks[m][3]
                act.wait_ge(mx_ready, m + 1)
                act.activation(sm[:, m % 2, 0:nk], sm[:, m % 2, 0:nk], ACT.Exp, bias=stat[:, m % 2, 1:2],
                               accum_out=stat[:, m % 2, 2:3]).then_inc(ex_ready, 1)

            exp_block(0)
            for m in range(len(blocks)):
                if m + 1 < len(blocks):
                    exp_block(m + 1)
                nk = blocks[m][3]
                ps = banks.full(act, ("pt", m))
                full, rest = divmod(nk, P)
                act.activation(p_t[:, m % 2, 0:full, :], ps[:, 0:full * P].rearrange("p (k n) -> p k n", k=full), ACT.Copy)
                act.activation(p_t[0:rest, m % 2, full, :], ps[0:rest, full * P:(full + 1) * P], ACT.Copy)\
                   .then_inc(banks.empty_sem(("pt", m)), 1)
            for t in range(TILES):
                rows = ROWS[t]
                copy(o_t[:, 0:4, t * P:t * P + rows], ("ogT", t), lambda ps: ps[:, 0:4 * rows].rearrange("p (h n) -> p h n", h=4))
            ln_rsqrt(0)
            for l in range(DEPTH):
                s = L[l]
                if l:
                    for c in range(0, DK_SLICES, 2):
                        copy(xt[:, c, 0:T_COLS], ("mx", c), lambda ps: ps[:, 0:T_COLS])
                    ln_rsqrt(2)
                copy_xt(l + 1)
                act.wait_ge(s["init"], 7 + l)
                act.wait_ge(x_ready, 3 + 6 * l)
                act.activation(xh[:, 0:2, :], x[:, 0:2, :], ACT.Copy)
                act.activation(xh[0:64, 2, :], x[0:64, 2, :], ACT.Copy).then_inc(s["x_split"], 1)
                ps = banks.full(act, ("lg", l))
                act.activation(sc[:, :, :], ps[:, 0:TILES * E].rearrange("p (t e) -> p t e", t=TILES), ACT.Exp, scale=-1.0)\
                   .then_inc(banks.empty_sem(("lg", l)), 1)
                for t in range(TILES):
                    rows = ROWS[t]
                    ps = banks.full(act, ("sg", l, t))
                    act.activation(sg[0:rows, :], ps[0:rows, 0:FE], ACT.Silu).then_inc(s["sg_sh"], 1)
                    copy(ht[:, :, 0:rows], ("shT", l, t), lambda ps: ps[:, 0:256].rearrange("p (k n) -> p k n", k=2)[:, :, 0:rows])
                    copy(acc[0:rows, t, 0:512], ("sd", l, t, 0), lambda ps: ps[0:rows, :])
                act_experts(act, l)
                ln_rsqrt(2 * l + 1)

        def dve_experts(dve, l, step):
            s = L[l]
            gu_b = banks.tile[0]
            rounds = dve.value_load(n_rounds[0:1, 0:1], min_val=1, max_val=MAX_ROUNDS)
            iota = bc(bc(const("iota"), 1, 4), 1, TILES)

            def pick_group(b, c0):
                dve.tensor_copy(wpick[:, b, :, :], wt_x[:, :, c0])
                dve.tensor_tensor(pick[b][:, :, :].rearrange("p t (e n) -> p t e n", e=4), iota,
                                  bc(pos_x[:, :, c0], 3, SLOTS), ALU.is_equal).then_inc(s["pick_ready"], 1)

            def copy_xg(b, u, n):
                dve.wait_ge(s["xg_done1"], n)
                dve.tensor_copy(xgt[b][:, 4 * u + 2:4 * u + 4, :], banks.tile[3][:, :].rearrange("p (k n) -> p k n", k=2))\
                   .then_inc(s["xg_copied1"], 1)

            def add_sums(n):
                for t in range(TILES):
                    rows = ROWS[t]
                    for c in range(2):
                        dst = acc[0:rows, t, c * 512:(c + 1) * 512]
                        dve.wait_ge(s[f"sum_done{c}"], n + t + 1)
                        dve.tensor_tensor(dst, dst, banks.tile[6 + c][0:rows, :], ALU.add).then_inc(s[f"added{c}"], 1)

            pick_group(0, slice(0, 4))
            for u in range(2):
                copy_xg(0, u, u + 1)
            banks.copied(dve, ("sd", l, TILES - 1, 0))
            banks.copied(dve, ("sd", l, TILES - 1, 1))
            with dve.Fori(0, rounds) as r:
                with dve.Fori(0, GROUPS // 2) as j:
                    for b in range(2):
                        for u in range(2):
                            n = r * GROUPS + 2 * j + b
                            i = 2 * n + u
                            if u == 0:
                                dve.wait_ge(s["place_done"], i + 1)
                                pick_group(1 - b, bass.ds(8 * j + 4 * b + 4, 4))
                            dve.wait_ge(s["sg_ready"], i + 1)
                            dve.tensor_tensor(hh[:, :], sg[:, :], gu_b[:, FE:2 * FE], ALU.mult).then_inc(s["h_ready"], 1)
                            copy_xg(1 - b, u, i + 3)
                            add_sums(3 * i)
                            for c in range(2):
                                dve.wait_ge(s[f"yh_ready{c}"], i + 1)
                                cc = slice(c * 512, (c + 1) * 512)
                                dve.scalar_tensor_tensor(out=yl[:, cc], in0=banks.tile[4 + c][:, :], scalar=gslot[:, u, :],
                                                         in1=yh[:, cc].bitcast(F32), op0=ALU.mult, op1=ALU.subtract)\
                                   .then_inc(s["y_ready"], 1)
                dve.tensor_scalar(pos_x[:, :, :], pos_x[:, :, :], -float(SLOTS), None, ALU.add).then_inc(s["next_round"], 1)
                dve.wait_ge(s["next_round"], r + 1)
            add_sums(3 * PAIRS * rounds)

        @block.vector
        def _(dve):
            step = Steps(dve, dve_step)

            def tt(dst, x0, x1, op, sem=None):
                step(dve.tensor_tensor(dst, x0, x1, op), sem)

            def ts(dst, x0, s1, s2, o1, o2=None, sem=None):
                step(dve.tensor_scalar(dst, x0, s1, s2, o1, o2) if o2 is not None else dve.tensor_scalar(dst, x0, s1, s2, o1), sem)

            def copy(dst, name, src):
                ps = banks.full(dve, name)
                dve.tensor_copy(dst, src(ps)).then_inc(banks.empty_sem(name), 1)

            def copy_xt(n):
                for i in range(1, 5, 2):
                    t, k0, nk = xt_part(i)
                    copy(xt_in_cols(i), ("xT", n, i), lambda ps: ps[:, 0:nk * ROWS[t]].rearrange("p (k n) -> p k n", k=nk))

            def layer_norm(n, before=None):
                for t in range(TILES):
                    rows = ROWS[t]
                    if before:
                        before(t, rows)
                    for c in range(2):
                        step(dve.bn_stats(ln_st[0:rows, t, c, :], x[0:rows, t, c * 512:(c + 1) * 512]))
                    step(dve.bn_aggr(ln_mv[0:rows, t, :], ln_st[0:rows, t, :, :].rearrange("p a b -> p (a b)")), var_ready)
                dve.wait_ge(ln_in, 32 * (n + 1))
                for t in range(TILES):
                    rows = ROWS[t]
                    xr = x[0:rows, t, :]
                    dve.wait_ge(rs_ready, 3 * n + t + 1)
                    ts(xr, xr, ln_mv[0:rows, t, 0:1], ln_rs[0:rows, t:t + 1], ALU.subtract, ALU.mult)
                    tt(xr, xr, ln_g[0:rows, :], ALU.mult)
                    tt(xr, xr, ln_b[0:rows, :], ALU.add, x_ready)

            copy_xt(0)
            for j in range(2):
                ps = banks.full(dve, ("qk", j))
                dve.tensor_scalar(q_t[:, j, :], ps[:, 0:T_COLS], GDK ** -0.5, None, ALU.mult).then_inc(banks.empty_sem(("qk", j)), 1)
            dve.wait_ge(mixp_in, 16 * MIX_PARAMS)
            for j in range(2):
                ps = banks.full(dve, ("z", j))
                step.banked(dve.tensor_scalar(z_t[:, j, :], ps[:, 0:T_COLS], bg[:, j:j + 1], None, ALU.add), banks, ("z", j))
            step(dve.tensor_copy(stat[:, 0, 0:2], bg[:, 0:2]), z_ready)
            step(dve.tensor_copy(stat[:, 0, 0:2], bg[:, 0:2]), z_ready)
            for t in range(TILES):
                rows = ROWS[t]
                copy(c_sb[0:rows, t, :], ("c", t), lambda ps: ps[0:rows, 0:416])
            dve.wait_ge(ls_ready, 1)
            for j in range(2):
                step(dve.scalar_tensor_tensor(out=z_t[:, j, :], in0=z_t[:, j, :], scalar=0.0, in1=u_t[:, j, :],
                                              op0=ALU.min, op1=ALU.subtract))
            ts(z_t[:, :, :], z_t[:, :, :], 1.0 / TAU, None, ALU.mult)
            dve.wait_ge(mix_in, 16)
            reset = mixc("scan")
            for j in range(2):
                step(dve.tensor_tensor_scan(b_t[:, j, :], reset, z_t[:, j, :], 0.0, ALU.mult, ALU.add),
                     b_ready if j else None)
            dve.wait_ge(zeroed, ZEROED)
            bm = b_t[:, :, 0:256].rearrange("p j (c t) -> p j c t", t=CHUNK)
            tt(kd_t[:, :, 0:256].rearrange("p j (c t) -> p j c t", t=CHUNK), bc(bm[:, :, :, CHUNK - 1], 3, CHUNK), bm, ALU.subtract)
            for c0, n in ((2 * P, TAIL), (SAMPLE0, N_DEC)):
                tt(kd_t[:, :, c0:c0 + n], bc(b_t[:, :, c0 + n - 1], 2, n), b_t[:, :, c0:c0 + n], ALU.subtract,
                   dk_ready if n == N_DEC else None)
            dve.wait_ge(eb_ready, 1)
            tt(qe_t[:, :, :], q_t[:, :, :], u_t[:, :, :], ALU.mult, qe_ready)
            dve.wait_ge(ek_ready, 1)
            for j in range(2, 4):
                banks.copied(dve, ("qk", j))
            tt(kd_t[:, :, :], kd_t[:, :, :], k_t[:, :, :], ALU.mult, qe_ready)
            dve.wait_ge(c_sq, 2)
            for t in range(TILES):
                rows = ROWS[t]
                step(dve.scalar_tensor_tensor(out=cq_n[0:rows, t, :], in0=c_sb[0:rows, t, 0:QL_R], scalar=mrs[0:rows, 0, t:t + 1],
                                              in1=g_q[0:rows, :], op0=ALU.mult, op1=ALU.mult))
                step(dve.scalar_tensor_tensor(out=ckv_n[0:rows, t, :], in0=c_sb[0:rows, t, QL_R:QL_R + KVL],
                                              scalar=mrs[0:rows, 1, t:t + 1], in1=g_kv[0:rows, :], op0=ALU.mult, op1=ALU.mult))
                cos, sin = (mixc(n)[0:rows, t * HALF:(t + 1) * HALF] for n in ("cos", "sin"))
                k1, k2 = (c_sb[0:rows, t, 384 + i:384 + i + HALF] for i in (0, HALF))
                r1, r2 = rot[0:rows, 0, 0:HALF], rot[0:rows, 1, 0:HALF]
                tt(r1, k1, cos, ALU.mult)
                tt(r2, k2, sin, ALU.mult)
                tt(kr[0:rows, t, 0:HALF], r1, r2, ALU.subtract)
                tt(r1, k1, sin, ALU.mult)
                tt(r2, k2, cos, ALU.mult)
                tt(kr[0:rows, t, HALF:], r1, r2, ALU.add, c_normed)
            dve.wait_ge(levels_zeroed, 1)
            for v in range(LEVELS):
                for j in range(2):
                    up, low = level_half(b_t[:, j, :], v, 1), level_half(b_t[:, j, :], v, 0)
                    ref = bc(low[:, :, (1 << v) - 1], 2, 1 << v)
                    dve.tensor_tensor(level_half(q_lev[:, v, j, :], v, 1), up, ref, ALU.subtract)
                    ins = dve.tensor_tensor(level_half(k_lev[:, v, j, :], v, 0), ref, low, ALU.subtract)
                    if j:
                        step(ins, lev_d)
            for v in range(LEVELS):
                dve.wait_ge(lev_e, v + 1)
                for j in range(2):
                    qh, kh = level_half(q_lev[:, v, j, :], v, 1), level_half(k_lev[:, v, j, :], v, 0)
                    dve.tensor_tensor(qh, qh, level_half(q_t[:, j, :], v, 1), ALU.mult)
                    ins = dve.tensor_tensor(kh, kh, level_half(k_t[:, j, :], v, 0), ALU.mult)
                    if j:
                        step(ins, lev_ready)
            for t in range(TILES):
                rows, n = ROWS[t], ("r", t)
                ps = banks.full(dve, n)
                dve.wait_ge(re_ready, t + 1)
                re = r_e[0:rows, :]
                ts(re, re, 1.0, None, ALU.add)
                step(dve.reciprocal(re, re))
                step.banked(dve.tensor_tensor(r_sb[0:rows, t, :], re, ps[0:rows, :], ALU.mult), banks, n)
            for t in range(TILES):
                rows, n = ROWS[t], ("qr", t)
                q = banks.full(dve, n)[0:rows, 0:256].rearrange("p (h r) -> p h r", h=MH)
                cos, sin = (bc(mixc(m)[0:rows, t * HALF:(t + 1) * HALF], 1, MH) for m in ("cos", "sin"))
                q1, q2 = q[:, :, 0:HALF], q[:, :, HALF:]
                r1, r2 = (rot[0:rows, i, :].rearrange("p (h r) -> p h r", h=MH) for i in range(2))
                o = q_rot[0:rows, t, :].rearrange("p (h r) -> p h r", h=MH)
                tt(r1, q1, cos, ALU.mult)
                tt(r2, q2, sin, ALU.mult)
                tt(o[:, :, 0:HALF], r1, r2, ALU.subtract)
                tt(r1, q1, sin, ALU.mult)
                step.banked(dve.tensor_tensor(r2, q2, cos, ALU.mult), banks, n)
                tt(o[:, :, HALF:], r1, r2, ALU.add, qrot_ready)
            dve.wait_ge(state_in, 16 * GH)
            for c, (t, pb, n) in enumerate(CHUNKS):
                levels = int(math.log2(n)) + 1
                w, table = (32, "gla_s") if n == 32 else (64, "gla")
                rows = slice(pb, pb + n)
                for h in range(GH):
                    name = ("att", c, h)
                    ps = banks.full(dve, name)
                    lv = lambda ap: ap[rows, 0:levels * w].rearrange("p (v t) -> p v t", v=levels)[:, :, 0:n]
                    step.banked(dve.tensor_tensor(lv(att_m), lv(ps), lv(mixc(table)), ALU.mult), banks, name)
                    step(dve.tensor_reduce(att[rows, t, h, 0:n], lv(att_m).rearrange("p v t -> p t v"), AX.X, ALU.add), att_ready)
                st = s_s if c == 5 else s_p
                for j in range(2):
                    copy(og[rows, t, j * 256:(j + 1) * 256], ("o", c, j), lambda ps: ps[rows, 0:256])
                    name = ("u", c, j)
                    ps = banks.full(dve, name)
                    last = t * P + pb + n - 1
                    for b in range(2):
                        hp, hc = slice(64 * b, 64 * b + 64), slice(128 * b, 128 * b + 128)
                        ins = dve.scalar_tensor_tensor(out=st[hp, j, hc], in0=st[hp, j, hc], scalar=u_t[hp, j, last:last + 1],
                                                       in1=ps[hp, hc], op0=ALU.mult, op1=ALU.add)
                        step.banked(ins, banks, name) if b else step(ins)
            for j in range(2):
                banks.copied(dve, ("o", 5, j))
            for t in range(TILES):
                rows = ROWS[t]
                tt(sq[0:rows, :], og[0:rows, t, :], og[0:rows, t, :], ALU.mult)
                step(dve.tensor_reduce(gss[0:rows, t * GH:(t + 1) * GH], sq[0:rows, :].rearrange("p (h n) -> p h n", h=GH),
                                       AX.X, ALU.add), gss_ready)
            dve.wait_ge(grs_ready, 1)
            for t in range(TILES):
                rows = ROWS[t]
                o = og[0:rows, t, :].rearrange("p (h n) -> p h n", h=GH)
                tt(o, o, bc(grs[0:rows, t * GH:(t + 1) * GH], 2, GDV), ALU.mult)
                tt(o, o, bc(g_gla[0:rows, :], 1, GH), ALU.mult)
                tt(og[0:rows, t, :], og[0:rows, t, :], r_sb[0:rows, t, :], ALU.mult, og_ready)
            blocks = attention_blocks()

            def scores(m):
                nk, mask = blocks[m][3], blocks[m][4]
                if m >= 2:
                    banks.full(dve, ("pt", m - 2))
                ps = banks.full(dve, ("s", m))
                row = sm[:, m % 2, 0:nk]
                step.banked(dve.scalar_tensor_tensor(out=row, in0=ps[:, 0:nk], scalar=MLA_SCALE, in1=mixc(mask)[:, 0:nk],
                                                     op0=ALU.mult, op1=ALU.add), banks, ("s", m))
                step(dve.tensor_reduce(stat[:, m % 2, 0:1], row, AX.X, ALU.max))
                ts(stat[:, m % 2, 1:2], stat[:, m % 2, 0:1], -1.0, None, ALU.mult, None, mx_ready)

            def latent_out(m):
                hs, q0, nq = blocks[m][:3]
                copy(q_lat[:, hs[0]:hs[-1] + 1, q0:q0 + nq], ("ol", m), lambda ps: ps[:, 0:P].rearrange("p (h n) -> p h n", h=len(hs)))

            scores(0)
            for m in range(len(blocks)):
                if m + 1 < len(blocks):
                    scores(m + 1)
                nk = blocks[m][3]
                dve.wait_ge(ex_ready, m + 1)
                step(dve.reciprocal(stat[:, m % 2, 3:4], stat[:, m % 2, 2:3]))
                ts(sm[:, m % 2, 0:nk], sm[:, m % 2, 0:nk], stat[:, m % 2, 3:4], None, ALU.mult, None, p_ready)
                if m:
                    latent_out(m - 1)
            latent_out(len(blocks) - 1)
            for g in range(4):
                copy(o_t[:, 4 + g, 0:T_COLS], ("om", g), lambda ps: ps[:, 0:T_COLS])

            def add_mixed(t, rows):
                for c in range(2):
                    n, xr = ("mo", t, c), x[0:rows, t, c * 512:(c + 1) * 512]
                    ps = banks.full(dve, n)
                    step.banked(dve.scalar_tensor_tensor(out=xr, in0=xr, scalar=ALPHA, in1=ps[0:rows, :],
                                                         op0=ALU.mult, op1=ALU.add), banks, n)

            layer_norm(0, add_mixed)
            for l in range(DEPTH):
                s = L[l]
                if l:
                    for c in range(1, DK_SLICES, 2):
                        copy(xt[:, c, 0:T_COLS], ("mx", c), lambda ps: ps[:, 0:T_COLS])

                    def add_pooled(t, rows):
                        for c in range(2):
                            n, cc = ("po", t, c), slice(c * 512, (c + 1) * 512)
                            ps = banks.full(dve, n)
                            step.banked(dve.tensor_tensor(acc[0:rows, t, cc], ps[0:rows, :], pool_s[0:rows, cc], ALU.mult), banks, n)
                        add_acc(t, rows)

                    dve.wait_ge(s["pool_in"], 16 * 4)

                def add_acc(t, rows):
                    step(dve.scalar_tensor_tensor(out=x[0:rows, t, :], in0=x[0:rows, t, :], scalar=ALPHA, in1=acc[0:rows, t, :],
                                                  op0=ALU.mult, op1=ALU.add))

                if l:
                    dve.wait_ge(stored, 16 * (MIX_STORES + 2))
                    layer_norm(2, add_pooled)
                copy_xt(l + 1)
                dve.wait_ge(rbias_in, 16 * DEPTH)
                dve.wait_ge(consts_in, 16)
                banks.copied(dve, ("lg", l))
                ts(sc[:, :, :], sc[:, :, :], 1.0, None, ALU.add)
                step(dve.reciprocal(sc[:, :, :], sc[:, :, :]))
                tt(bi[:, :, :], sc[:, :, :], bc(rbias[:, l, :], 1, TILES), ALU.add)
                b4 = bi[:, :, :].rearrange("p t (g n) -> p t g n", g=NG)
                tt(g_a[:, :, :, :], b4[:, :, :, 0:4], b4[:, :, :, 4:8], ALU.max)
                tt(g_b[:, :, :, :], b4[:, :, :, 0:4], b4[:, :, :, 4:8], ALU.min)
                for w in (2, 1):
                    a0, a1 = g_a[:, :, :, 0:w], g_a[:, :, :, w:2 * w]
                    b0, b1 = g_b[:, :, :, 0:w], g_b[:, :, :, w:2 * w]
                    tt(g_c[:, :, :, 0:w], a0, a1, ALU.min)
                    tt(a0, a0, a1, ALU.max)
                    tt(b0, b0, b1, ALU.max)
                    tt(b0, b0, g_c[:, :, :, 0:w], ALU.max)
                tt(gs[:, :, :], g_a[:, :, :, 0], g_b[:, :, :, 0], ALU.add)
                for t in range(TILES):
                    other, own = bc(gs[:, t, :], 1, NG), bc(gs[:, t, :], 2, NG)
                    tt(cmp1[:, t, :, :], other, own, ALU.is_gt)
                    tt(cmp2[:, t, :, :], other, own, ALU.is_equal)
                    tt(cmp2[:, t, :, :], cmp2[:, t, :, :], const("lower_group").rearrange("p (g n) -> p g n", g=NG), ALU.mult)
                tt(cmp1[:, :, :, :], cmp1[:, :, :, :], cmp2[:, :, :, :], ALU.add)
                step(dve.tensor_reduce(rank[:, :, :], cmp1[:, :, :, :], AX.X, ALU.add))
                ts(rank[:, :, :], rank[:, :, :], float(TOPG), None, ALU.is_lt)
                m4 = mk[:, :, :].rearrange("p t (g n) -> p t g n", g=NG)
                tt(m4, b4, bc(rank[:, :, :], 3, E // NG), ALU.mult)
                ts(rank[:, :, :], rank[:, :, :], 1.0, BIG, ALU.subtract, ALU.mult)
                tt(m4, m4, bc(rank[:, :, :], 3, E // NG), ALU.add)
                for t in range(TILES):
                    step(dve.max(mx8[:, t, :], mk[:, t, :]))
                    step(dve.match_replace(mr[:, t, :], in_to_replace=mx8[:, t, :], in_values=mk[:, t, :], imm_value=-BIG))
                tt(sel[:, :, :], mr[:, :, :], mk[:, :, :], ALU.not_equal)
                tt(tmp[:, :, :], sc[:, :, :], sel[:, :, :], ALU.mult)
                step(dve.tensor_reduce(wsum[:, :], tmp[:, :, :], AX.X, ALU.add))
                step(dve.reciprocal(wsum[:, :], wsum[:, :]))
                ts(wsum[:, :], wsum[:, :], ROUTED_SCALE, None, ALU.mult)
                tt(wt_x[:, :, 0:E], tmp[:, :, :], bc(wsum[:, :], 2, E), ALU.mult)
                valid = bc(const("valid"), 2, E)
                tt(wt_x[:, :, 0:E], wt_x[:, :, 0:E], valid, ALU.mult)
                step(dve.tensor_copy(wt_x[:, :, E:], wt_x[:, :, 0:4]))
                tt(sel[:, :, :], sel[:, :, :], valid, ALU.mult, s["sel_ready"])
                dve.wait_ge(s["x_split"], 1)
                dve.tensor_tensor(xl[:, 0:2, :], x[:, 0:2, :], xh[:, 0:2, :].bitcast(F32), ALU.subtract)
                dve.tensor_tensor(xl[0:64, 2, :], x[0:64, 2, :], xh[0:64, 2, :].bitcast(F32), ALU.subtract).then_inc(s["x_split"], 1)
                n = ("pos", l)
                ps = banks.full(dve, n)
                ps3 = ps[:, 0:TILES * E].rearrange("p (t e) -> p t e", t=TILES)
                step(dve.tensor_scalar(pos_x[:, :, 0:E], ps3, 1.0, None, ALU.add))
                step.banked(dve.tensor_copy(cnt[:, :], ps[:, TILES * E:(TILES + 1) * E]), banks, n)
                tt(pos_x[:, :, 0:E], pos_x[:, :, 0:E], sel[:, :, :], ALU.mult)
                ts(pos_x[:, :, 0:E], pos_x[:, :, 0:E], -1.0, None, ALU.add)
                ts(pos_x[:, :, E:], pos_x[:, :, 0:4], -float(SLOTS), None, ALU.add)
                step(dve.tensor_reduce(cmax[:, :], cnt[:, :], AX.X, ALU.max))
                ts(thr_c[:, :], const("thr"), cmax[:, 0:1], None, ALU.is_lt)
                step(dve.tensor_reduce(cmax[:, :], thr_c[:, :], AX.X, ALU.add))
                ts(n_rounds[:, :], cmax[:, :], 1.0, None, ALU.add, None, s["rounds_ready"])
                for t in range(TILES):
                    rows, n = ROWS[t], ("sg", l, t)
                    ps = banks.full(dve, n)
                    dve.wait_ge(s["sg_sh"], t + 1)
                    step.banked(dve.tensor_tensor(hh[0:rows, :], sg[0:rows, :], ps[0:rows, FE:2 * FE], ALU.mult), banks, n)
                    copy(acc[0:rows, t, 512:D], ("sd", l, t, 1), lambda ps: ps[0:rows, :])
                dve_experts(dve, l, step)
                layer_norm(2 * l + 1, add_acc)


_OUTS = [("y_prompt", (1, SEQ, D)), ("y_sample", (1, N_DEC, D)),
         ("prompt_ckv", (1, N_PROMPT, KVL)), ("prompt_krope", (1, N_PROMPT, ROPE)),
         ("prompt_gla_state", (1, GH, GDK, GDV)), ("prompt_pool_rows", (1, 15, D)),
         ("sample_ckv", (1, N_DEC, KVL)), ("sample_krope", (1, N_DEC, ROPE)),
         ("sample_gla_state", (1, GH, GDK, GDV)), ("sample_pool_rows", (1, 15, D))]


def kernel(**inputs):
    import concourse.bacc as _bacc
    from concourse.bass_utils import run_bass_kernel_spmd as _run

    nc = _bacc.Bacc("TRN2", target_bir_lowering=False, num_devices=1)
    tables = dict(zip(("cst", "mix", "band"), constants()))
    arrays, a = {}, {}
    for name, v in {**inputs, **tables}.items():
        v = np.ascontiguousarray(v)
        arrays[f"in_{name}_dram"] = v
        a[name] = nc.dram_tensor(f"in_{name}_dram", v.shape, mybir.dt.from_np(v.dtype), kind="ExternalInput").ap()
    a["outs"] = {n: nc.dram_tensor(f"out_{n}_dram", shape, F32, kind="ExternalOutput").ap() for n, shape in _OUTS}
    build(nc, a)
    r = _run(nc, [arrays], core_ids=[0])
    return tuple(r.results[0][f"out_{n}_dram"] for n, _ in _OUTS)
```

```python
import math
from contextlib import ExitStack

import numpy as np

import concourse.bass as bass
from concourse import mybir

F32 = mybir.dt.float32
F32R = mybir.dt.float32r
I32 = mybir.dt.int32
ALU = mybir.AluOpType
ACT = mybir.ActivationFunctionType
AX = mybir.AxisListType

P = 128
D = 1024
SEQ, N_META, N_DEC, PAST = 256, 16, 32, 256
N_PROMPT = N_META + SEQ
N_KEYS_PAST = N_META + PAST
DEPTH = 2
ALPHA = float((2 * DEPTH) ** 0.25)
LN_EPS, RMS_EPS = 1e-5, 1e-6
NEG = -1e30

DK_SLICES = D // P
TILES = 3
ROWS = [128, 128, 64]
SAMPLE_ROW = 32
SAMPLE0 = 2 * P + SAMPLE_ROW
TAIL = N_PROMPT - 2 * P
T_COLS = 320
T_PAD = TILES * P

GH, GDK, GDV, GRANK = 4, 64, 128, 16
CHUNK = 64
TAU = 16.0
CHUNKS = [(0, 0, 64), (0, 64, 64), (1, 0, 64), (1, 64, 64), (2, 0, TAIL), (2, SAMPLE_ROW, N_DEC)]
LEVELS = 6
CHUNKS_BY_TILE = [[0], [1], [5, 2, 3, 4]]

MH, QL_R, KVL, NOPE, ROPE, MV = 8, 256, 128, 64, 32, 64
MLA_SCALE = float((NOPE + ROPE) ** -0.5)
HALF = ROPE // 2
S_KEYS = 320

C_Q, C_K, C_V, C_R = 0, 256, 512, 1024
C_A, C_CQ, D_IN = 1536, 1552, 1968

E, FE, TOPG, NG, TOPK = 64, 256, 4, 8, 8
ROUTED_SCALE = 2.5
PAIRS = E // 2
GROUPS = PAIRS // 2
SLOTS = 64
ZEROED = 2 + 9 + 2
MIX_PARAMS = 11
MIX_STORES = 6 + 2 * GH
MAX_ROUNDS = -(-(N_PROMPT + N_DEC) // SLOTS)
BIG = 3e38
WIN = (2, 4, 8, 16)
PG = 256


def layout(widths):
    at, out = 0, {}
    for name, w in widths:
        out[name] = (at, at + w)
        at += w
    return out, at


CST, CST_W = layout([("ident", 128), ("before", 128), ("ones", 128), ("iota", SLOTS), ("valid", TILES),
                     ("thr", MAX_ROUNDS - 1), ("lower_group", NG * NG)])
MIX, MIX_W = layout([("gla", (LEVELS + 1) * 64), ("mask0", 144), ("mask1", N_PROMPT),
                     ("mask_s", S_KEYS), ("scan", T_COLS), ("cos", TILES * HALF), ("sin", TILES * HALF)])
BAND, BAND_W = layout([("own0", 4 * 128), ("own1", 4 * 128), ("prev1", 4 * 128), ("own2", 4 * 64),
                       ("prev2", 4 * 64), ("cache", 4 * 64)])


def constants():
    f = np.float32
    p = np.arange(P)
    cst = np.zeros((P, CST_W), f)
    put = lambda a, tab, n, v: a.__setitem__((slice(None), slice(*tab[n])), np.asarray(v, f).reshape(a.shape[0], -1))
    put(cst, CST, "ident", np.eye(P))
    put(cst, CST, "before", p[:, None] < p[None, :])
    put(cst, CST, "ones", np.ones((P, P)))
    put(cst, CST, "iota", np.tile(np.arange(SLOTS), (P, 1)))
    valid = np.ones((P, TILES))
    valid[:, 2] = (p < TAIL) | ((p >= SAMPLE_ROW) & (p < SAMPLE_ROW + N_DEC))
    put(cst, CST, "valid", valid)
    put(cst, CST, "thr", np.tile(SLOTS * np.arange(1, MAX_ROUNDS), (P, 1)))
    g = np.arange(NG)
    put(cst, CST, "lower_group", np.tile((g[None, :] < g[:, None]).reshape(1, -1), (P, 1)))

    mix = np.zeros((P, MIX_W), f)

    def level_masks(s, t):
        out = [s[:, None] == t[None, :]]
        for l in range(LEVELS):
            b, h = 2 << l, 1 << l
            out.append((s[:, None] // b == t[None, :] // b) & (s[:, None] % b < h) & (t[None, :] % b >= h))
        return np.stack(out, 1)

    put(mix, MIX, "gla", level_masks(p % 64, np.arange(64)))
    pos = np.arange(N_PROMPT)
    chunk = np.where(pos < N_META, -1, (pos - N_META) // CHUNK)
    seen = lambda q, k: np.where(chunk[:k][None, :] <= chunk[q][:, None], 0.0, NEG)
    put(mix, MIX, "mask0", seen(p, 144))
    put(mix, MIX, "mask1", seen(P + p, N_PROMPT))
    ks = np.arange(S_KEYS)
    put(mix, MIX, "mask_s", np.tile(np.where((ks >= N_KEYS_PAST) & (ks < SAMPLE0), NEG, 0.0), (P, 1)))
    cols = np.arange(T_COLS)
    put(mix, MIX, "scan", np.tile((cols % CHUNK != 0) & (cols != SAMPLE0), (P, 1)))
    tok = np.arange(T_PAD)
    tpos = np.where(tok < SAMPLE0, tok, N_META + PAST + tok - SAMPLE0).astype(f)
    inv = (f(10000.0) ** (-np.arange(HALF, dtype=f) / f(HALF))).astype(f)
    ang = (tpos[:, None] * inv).astype(f)
    put(mix, MIX, "cos", np.cos(ang).reshape(TILES, P, HALF).transpose(1, 0, 2))
    put(mix, MIX, "sin", np.sin(ang).reshape(TILES, P, HALF).transpose(1, 0, 2))

    band = np.zeros((P, BAND_W), f)
    full = np.zeros((4, T_PAD, T_PAD))
    cache = np.zeros((4, P, T_PAD))
    for gi, w in enumerate(WIN):
        for t in range(N_PROMPT):
            lo = max(t + 1 - w, 0)
            full[gi, lo:t + 1, t] = 1.0 / (t + 1 - lo)
            full[gi, t, t] -= 1.0
        for i in range(N_DEC):
            for j in range(i + 1 - w, i + 1):
                if j >= 0:
                    full[gi, SAMPLE0 + j, SAMPLE0 + i] += 1.0 / w
                else:
                    cache[gi, 15 + j, SAMPLE0 + i] = 1.0 / w
            full[gi, SAMPLE0 + i, SAMPLE0 + i] -= 1.0
    tr = lambda a: a.transpose(1, 0, 2)
    put(band, BAND, "own0", tr(full[:, 0:128, 0:128]))
    put(band, BAND, "own1", tr(full[:, 128:256, 128:256]))
    put(band, BAND, "prev1", tr(full[:, 0:128, 128:256]))
    put(band, BAND, "own2", tr(full[:, 256:384, 256:320]))
    put(band, BAND, "prev2", tr(full[:, 128:256, 256:320]))
    put(band, BAND, "cache", tr(cache[:, :, 256:320]))
    return cst, mix, band


class Banks:

    def __init__(self, nc, ctx, names):
        self.tile = [ctx.enter_context(nc.psum_tensor(f"bank{b}", [P, 512], F32)) for b in range(8)]
        self.filled = [ctx.enter_context(nc.semaphore(f"filled{b}")) for b in range(8)]
        self.emptied = [ctx.enter_context(nc.semaphore(f"emptied{b}")) for b in range(8)]
        self.order = names
        assert len(set(names)) == len(names)
        self.at = {n: (i % 8, i // 8) for i, n in enumerate(names)}
        self.next = 0

    def ap(self, name):
        return self.tile[self.at[name][0]]

    def open(self, pe, name):
        assert self.order[self.next] == name, (self.order[self.next], name)
        self.next += 1
        b, n = self.at[name]
        if n:
            pe.wait_ge(self.emptied[b], n)
        return self.tile[b]

    def full(self, eng, name):
        b, n = self.at[name]
        eng.wait_ge(self.filled[b], n + 1)
        return self.tile[b]

    def fill_sem(self, name):
        return self.filled[self.at[name][0]]

    def empty_sem(self, name):
        return self.emptied[self.at[name][0]]

    def copied(self, eng, name):
        b, n = self.at[name]
        eng.wait_ge(self.emptied[b], n + 1)

    def all_copied(self, eng, name):
        i = self.order.index(name)
        for b in range(8):
            n = sum(1 for k in range(i + 1) if k % 8 == b)
            if n:
                eng.wait_ge(self.emptied[b], n)


def bank_uses():
    u = [("xT", 0, i) for i in range(5)]
    u += [("qk", j) for j in range(4)] + [("a",)] + [("z", j) for j in range(2)]
    u += [("c", t) for t in range(TILES)] + [("v", t) for t in range(TILES)] + [("r", j) for j in range(4)]
    u += [("mT", t) for t in range(TILES)] + [("pT", g) for g in range(TILES)] + [("ukT",)]
    u += [("qn", g) for g in range(4)] + [("qr", t) for t in range(TILES)]
    u += [("kd", t) for t in range(TILES)]
    for t in range(TILES):
        u += [("att", t, h) for h in range(GH)]
        if t == 0:
            u += [("ql", h) for h in range(MH)]
        if t == 1:
            u += [("qrT", i) for i in range(5)]
        for c in CHUNKS_BY_TILE[t]:
            u += [x for j in range(2) for x in (("o", c, j), ("u", c, j))]
    n = len(attention_blocks())
    for i in range(n + 3):
        u += [("s", i)] if i < n else []
        u += [("pt", i - 2)] if 0 <= i - 2 < n else []
        u += [("ol", i - 3)] if 0 <= i - 3 < n else []
    u += [("ogT", t) for t in range(TILES)] + [("om", g) for g in range(4)]
    u += [("mo", t, c) for t in range(TILES) for c in range(2)]
    for l in range(DEPTH):
        if l:
            u += [("mx", c) for c in range(DK_SLICES)] + [("po", t, c) for t in range(TILES) for c in range(2)]
        u += [("xT", l + 1, i) for i in range(5)]
        u += [("lg", l)] + [(n, l, b) for b in range(2) for n in ("sg", "su")] + [("pos", l)]
        u += [("sd", l, t, c) for t in range(TILES) for c in range(2)]
    return u


def attention_blocks():
    out = []
    for h in range(MH):
        out += [([h], 0, 128, 144, "mask0", False), ([h], 128, 128, N_PROMPT, "mask1", False)]
    out.append((list(range(MH)), 2 * P, TAIL, N_PROMPT, "mask_s", False))
    for b in range(2):
        out.append((list(range(4 * b, 4 * b + 4)), SAMPLE0, N_DEC, S_KEYS, "mask_s", True))
    return out


class Steps:

    def __init__(self, eng, sem):
        self.eng, self.sem, self.counts = eng, sem, {}

    def __call__(self, ins, sem=None):
        sem = self.sem if sem is None else sem
        n = self.counts[id(sem)] = self.counts.get(id(sem), 0) + 1
        ins.then_inc(sem, 1)
        self.eng.wait_ge(sem, n)

    def banked(self, ins, banks, name):
        ins.then_inc(banks.empty_sem(name), 1)
        banks.copied(self.eng, name)


def second(t, half):
    return slice(64 * half, 64 * half + 64) if t == 2 else slice(0, P)


def xt_part(i):
    return (i // 2, 4 * (i % 2), 4) if i < 4 else (2, 0, 8)


def bc(ap, axis, n):
    a = ap.unsqueeze(axis)
    shape = list(a.shape)
    shape[axis] = n
    return a.broadcast_to(shape)


def build(nc, a):
    out = a["outs"]
    ctx = ExitStack()
    with ctx:
        mixer_ctx, moe_ctx = ExitStack(), ExitStack()

        def sb(name, shape, dt=F32, scope=ctx):
            return scope.enter_context(nc.sbuf_tensor(f"sb_{name}", shape, dt))

        def sem(name):
            return ctx.enter_context(nc.semaphore(name))

        x = sb("x", [P, TILES, D])
        xt = sb("xt", [P, DK_SLICES, T_PAD])
        cst = sb("cst", [P, CST_W])
        ln_g = sb("ln_g", [P, D])
        ln_b = sb("ln_b", [P, D])
        rbias = sb("rbias", [P, DEPTH, E])
        ln_st = sb("ln_st", [P, TILES, 2, 6])
        ln_mv = sb("ln_mv", [P, TILES, 2])
        ln_rs = sb("ln_rs", [P, TILES])
        eps = sb("eps", [P, 2])

        def const(name):
            return cst[:, slice(*CST[name])]

        def mb(name, shape, dt=F32):
            return sb(name, shape, dt, mixer_ctx)

        q_t = mb("q_t", [P, 2, T_COLS])
        k_t = mb("k_t", [P, 2, T_COLS])
        b_t = mb("b_t", [P, 2, T_COLS])
        u_t = mb("u_t", [P, 2, T_COLS])
        qe_t = mb("qe_t", [P, 2, T_COLS])
        kd_t = mb("kd_t", [P, 2, T_COLS])
        c_sb = mb("c", [P, TILES, 416])
        att = mb("att", [P, TILES, GH, 64])
        att_m = mb("att_m", [P, (LEVELS + 1) * 64])
        kd = mb("kd", [P, TILES, 256])
        w_lo = mb("w_in_lo", [P, 8 * 1024])
        w_hi = mb("w_in_hi", [P, 8 * 1024])
        w_qk = w_lo[:, 0:8 * 512].rearrange("p (k n) -> p k n", k=8)
        w_ac = w_lo[:, 4096:4096 + 8 * 432].rearrange("p (k n) -> p k n", k=8)
        w_v = w_hi[:, 0:4096].rearrange("p (k n) -> p k n", k=8)
        w_r = w_hi[:, 4096:8192].rearrange("p (k n) -> p k n", k=8)
        w_out = w_lo[:, :].rearrange("p (k n) -> p k n", k=8)
        half = LEVELS * 2 * T_COLS
        q_lev = w_lo[:, 0:half].rearrange("p (l j t) -> p l j t", l=LEVELS, j=2)
        k_lev = w_lo[:, half:2 * half].rearrange("p (l j t) -> p l j t", l=LEVELS, j=2)
        few = MH * (TAIL + N_DEC)
        parts, _ = layout([("q_lat", 8 * T_COLS), ("q_rot_t", 8 * T_COLS), ("sm", 4 * T_COLS), ("p_t", 2 * TILES * P),
                           ("q_few", few), ("q_few_rot", few)])
        hi = {n: w_hi[:, slice(*parts[n])] for n in parts}
        q_lat = hi["q_lat"].rearrange("p (h t) -> p h t", h=8)
        q_rot_t = hi["q_rot_t"].rearrange("p (h t) -> p h t", h=8)
        q_few = hi["q_few"]
        q_few_rot = hi["q_few_rot"][0:ROPE, :]
        sm = hi["sm"].rearrange("p (b t) -> p b t", b=4)
        p_t = hi["p_t"].rearrange("p (b k n) -> p b k n", b=2, k=TILES)
        mix = mb("mix", [P, MIX_W])
        v_sb = mb("v", [P, TILES, 512])
        r_t = mb("r_t", [P, 4, T_COLS])
        og = mb("og", [P, TILES, 512])
        z_t = mb("z_t", [P, 2, T_COLS])
        a_t = mb("a_t", [GRANK, T_COLS])
        sq = mb("sq", [P, 512])
        wg2 = mb("wg2", [GRANK, 256])
        bg = mb("bg", [P, 2])
        g_gla = mb("g_gla", [P, GDV])
        g_q = mb("g_q", [P, QL_R])
        g_kv = mb("g_kv", [P, KVL])
        w_uqn = mb("w_uqn", [P, 2, MH, NOPE])
        w_uqr = mb("w_uqr", [P, 2, MH, ROPE])
        w_uk = mb("w_uk", [P, 512])
        w_uv = mb("w_uv", [P, MH, MV])
        uk_t = mb("uk_t", [P, 4, 128])
        cq_n = mb("cq_n", [P, TILES, QL_R])
        ckv_n = mb("ckv_n", [P, TILES, KVL])
        kr = mb("kr", [P, TILES, ROPE])
        rot = mb("rot", [P, 2, 128])
        cq_t = mb("cq_t", [P, 2, T_COLS])
        kv_t = mb("kv_t", [P, T_COLS])
        kr_t = mb("kr_t", [ROPE, T_COLS])
        skv_t = mb("skv_t", [P, S_KEYS])
        skr_t = mb("skr_t", [ROPE, S_KEYS])
        past = mb("past", [P, TILES, KVL])
        past_r = mb("past_r", [P, TILES, ROPE])
        q_n_t = mb("q_n_t", [P, 4, T_COLS])
        q_rot = mb("q_rot", [P, TILES, 256])
        msq = mb("msq", [P, 2, 4])
        mrs = mb("mrs", [P, 2, 4])
        s_p = mb("s_p", [P, 2, 256])
        s_s = mb("s_s", [P, 2, 256])
        gss = mb("gss", [P, TILES * GH])
        grs = mb("grs", [P, TILES * GH])
        stat = mb("stat", [P, 4, 4])
        mixer_ctx.close()
        o_t = xt

        def eb(name, shape, dt=F32):
            return sb(name, shape, dt, moe_ctx)

        w_rt = eb("w_rt", [P, 8, E])
        wslot = [eb(f"wslot{u}", [P, 12288]) for u in (1, 0)][::-1]
        w_gate = [w[:, 4096:8192].rearrange("p (e n) -> p e n", e=2) for w in wslot]
        w_up = [w[:, 8192:12288].rearrange("p (e n) -> p e n", e=2) for w in wslot]
        w_gu = [w[:, 4096:12288].rearrange("p (m e n) -> p m e n", m=2, e=2) for w in wslot]
        w_down = [w[:, 0:4096].rearrange("p (e n) -> p e n", e=2) for w in wslot]
        sh_gate = wslot[1][:, 0:2048].rearrange("p (k n) -> p k n", k=8)
        sh_up = wslot[1][:, 2048:4096].rearrange("p (k n) -> p k n", k=8)
        sh_down = wslot[1][:, 4096:6144].rearrange("p (k n) -> p k n", k=2)
        pool_w = wslot[1][:, 6144:8192].rearrange("p (g k n) -> p g k n", g=4, k=2)
        pool_s = wslot[1][:, 8192:9216]
        band = wslot[1][:, 9216:9216 + BAND_W]
        acc = eb("acc", [P, TILES, D])
        xh = eb("xh", [P, TILES, D], F32R)
        xl = eb("xl", [P, 2, D], F32R)
        yh = eb("yh", [P, D], F32R)
        yl = eb("yl", [P, D], F32R)
        xg_own = eb("xg_own", [P, DK_SLICES * 2 * P])
        xgt = [ap.rearrange("p (k n) -> p k n", k=DK_SLICES) for ap in
               (xg_own[:, :], xt[:, :, :].rearrange("p k n -> p (k n)")[:, 0:DK_SLICES * 2 * P])]
        pool_c = xg_own[:, 0:D]
        pick = [eb(f"pick{b}", [P, TILES, 2 * P], F32R) for b in range(2)]
        wpick = eb("wpick", [P, 2, TILES, 4])
        place = [eb(f"place{u}", [P, T_PAD], F32R) for u in range(2)]
        gslot = eb("gslot", [P, 2, 1])
        sg = eb("sg", [P, FE])
        hh = eb("hh", [P, FE])
        ht = eb("ht", [P, 2, P])
        sh_sg = xg_own[:, 0:2 * T_COLS].rearrange("p (b t) -> p b t", b=2)
        sh_h = xg_own[:, 2 * T_COLS:4 * T_COLS].rearrange("p (b t) -> p b t", b=2)
        sc = eb("sc", [P, TILES, E])
        bi = eb("bi", [P, TILES, E])
        mk = eb("mk", [P, TILES, E])
        mr = eb("mr", [P, TILES, E])
        sel = eb("sel", [P, TILES, E])
        tmp = eb("tmp", [P, TILES, E])
        mx8 = eb("mx8", [P, TILES, 8])
        g_a = eb("g_a", [P, TILES, NG, 4])
        g_b = eb("g_b", [P, TILES, NG, 4])
        g_c = eb("g_c", [P, TILES, NG, 2])
        gs = eb("gs", [P, TILES, NG])
        cmp1 = eb("cmp1", [P, TILES, NG, NG])
        cmp2 = eb("cmp2", [P, TILES, NG, NG])
        rank = eb("rank", [P, TILES, NG])
        wsum = eb("wsum", [P, TILES])
        pos_x = eb("pos_x", [P, TILES, E + 4])
        wt_x = eb("wt_x", [P, TILES, E + 4])
        cnt = eb("cnt", [P, E])
        cmax = eb("cmax", [P, 1])
        thr_c = eb("thr_c", [P, MAX_ROUNDS - 1])
        n_rounds = eb("n_rounds", [P, 1], I32)
        moe_ctx.close()

        def mixc(name):
            return mix[:, slice(*MIX[name])]

        def level_half(ap, v, part):
            b = 2 << v
            n = 4 * CHUNK if b == CHUNK else T_COLS
            h = 1 << v
            return ap[:, 0:n].rearrange("p (m t) -> p m t", t=b)[:, :, part * h:(part + 1) * h]

        banks = Banks(nc, ctx, bank_uses())

        consts_in = sem("consts_in")
        mix_in = sem("mix_in")
        rbias_in = sem("rbias_in")
        y_stored = sem("y_stored")
        x_zeroed = sem("x_zeroed")
        x_in = sem("x_in")
        w_in = [sem(f"w_in{i}") for i in range(4)]
        mixp_in = sem("mixp_in")
        past_in = sem("past_in")
        state_in = sem("state_in")
        w_out_in = sem("w_out_in")
        zeroed = sem("zeroed")
        levels_zeroed = sem("levels_zeroed")
        ln_in = sem("ln_in")
        stored = sem("stored")
        dve_step = sem("dve_step")
        act_step = sem("act_step")
        z_ready = sem("z_ready")
        ls_ready = sem("ls_ready")
        b_ready = sem("b_ready")
        eb_ready = sem("eb_ready")
        dk_ready = sem("dk_ready")
        ek_ready = sem("ek_ready")
        lev_d = sem("lev_d")
        lev_e = sem("lev_e")
        lev_ready = sem("lev_ready")
        qe_ready = sem("qe_ready")
        c_sq = sem("c_sq")
        c_normed = sem("c_normed")
        att_ready = sem("att_ready")
        state_ready = sem("state_ready")
        qrot_ready = sem("qrot_ready")
        skeys_ready = sem("skeys_ready")
        gss_ready = sem("gss_ready")
        grs_ready = sem("grs_ready")
        og_ready = sem("og_ready")
        mx_ready = sem("mx_ready")
        ex_ready = sem("ex_ready")
        p_ready = sem("p_ready")
        x_pre = sem("x_pre")
        var_ready = sem("var_ready")
        rs_ready = sem("rs_ready")
        x_ready = sem("x_ready")
        L = [{n: sem(f"{n}_{l}") for n in (
            "router_in", "shared_in", "pool_c_in", "gu_in0", "gu_in1", "down_in0", "down_in1", "pool_in", "x_split",
            "lg_exp", "sel_ready", "rounds_ready", "init",
            "gu_done0", "gu_done1", "down_done0", "down_done1", "xg_done0", "xg_done1", "xg_copied0", "xg_copied1",
            "pick_ready", "sg_ready", "h_ready", "ht_done", "ht_copied", "place_done", "place_copied",
            "yh_ready0", "yh_ready1", "yl_ready0", "yl_ready1", "sum_done0", "sum_done1", "added0", "added1",
            "y_ready", "next_round")} for l in range(DEPTH)]

        act_gate = [sem(f"act_gate{l}") for l in range(DEPTH)]

        block = ctx.enter_context(nc.Block())

        def load_pair(sp, l, u, pair, parts):
            two = bass.ds(pair * 2, 2) if not isinstance(pair, int) else slice(2 * pair, 2 * pair + 2)
            for name, dst in parts:
                src = a[f"moe_w_{name}"][l][two, :, :]
                src = src.rearrange("e (p k) f -> p e (k f)", p=P)
                sp.dma_start(dst[u], src).then_inc(L[l][f"{'down' if name == 'down' else 'gu'}_in{u}"], 16)

        GU = [("gate", w_gate), ("up", w_up)]
        DN = [("down", w_down)]

        def load_shared(sp, l):
            s = L[l]
            sp.dma_start(w_rt[:, :, :], a["moe_router_w"][l].rearrange("(p k) e -> p k e", k=8)).then_inc(s["router_in"], 16)
            for name, dst in (("gate", sh_gate), ("up", sh_up), ("down", sh_down)):
                k = dst.shape[1]
                sp.dma_start(dst, a[f"moe_sh_{name}"][l].rearrange("(p k) f -> p k f", k=k)).then_inc(s["shared_in"], 16)

        def sp_experts(sp, l):
            s = L[l]
            if l == 0:
                load_pair(sp, l, 0, 0, GU)
                load_pair(sp, l, 0, 0, DN)
            if l == 1:
                banks.full(sp, ("po", TILES - 1, 1))
                for t in range(TILES):
                    for c in range(2):
                        banks.copied(sp, ("po", t, c))
            load_pair(sp, l, 1, 1, GU[1:])
            banks.full(sp, ("su", l, 1))
            load_pair(sp, l, 1, 1, DN)
            banks.full(sp, ("sd", l, TILES - 1, 1))
            load_pair(sp, l, 1, 1, GU[:1])
            with sp.Fori(1, GROUPS) as j:
                for u in range(2):
                    sp.wait_ge(s[f"gu_done{u}"], j)
                    load_pair(sp, l, u, 2 * j + u, GU)
                    sp.wait_ge(s[f"down_done{u}"], j)
                    load_pair(sp, l, u, 2 * j + u, DN)
            sp.wait_ge(s["rounds_ready"], 1)
            rounds = sp.value_load(n_rounds[0:1, 0:1], min_val=1, max_val=MAX_ROUNDS)
            with sp.If(rounds - 1):
                with sp.Fori(1, rounds) as r:
                    with sp.Fori(0, GROUPS) as j:
                        for u in range(2):
                            sp.wait_ge(s[f"gu_done{u}"], r * (GROUPS) + j)
                            load_pair(sp, l, u, 2 * j + u, GU)
                            sp.wait_ge(s[f"down_done{u}"], r * (GROUPS) + j)
                            load_pair(sp, l, u, 2 * j + u, DN)
            if l == 0:
                uses = rounds * GROUPS
                sp.wait_ge(s["gu_done0"], uses)
                load_pair(sp, 1, 0, 0, GU)
                sp.wait_ge(s["down_done0"], uses)
                load_pair(sp, 1, 0, 0, DN)
                sp.wait_ge(s["gu_done1"], uses)
                n = L[1]["pool_in"]
                sp.dma_start(band, a["band"]).then_inc(n, 16)
                sp.dma_start(pool_w, a["pool_w"].rearrange("g (k p) n -> p g k n", p=P)).then_inc(n, 16)
                sp.dma_start(pool_s, a["pool_scale"].partition_broadcast(P)).then_inc(n, 16)
                sp.wait_ge(s["down_done1"], uses)
                load_shared(sp, 1)

        def xt_in_cols(i):
            t, k0, nk = xt_part(i)
            return xt[:, k0:k0 + nk, t * P:t * P + ROWS[t]]

        @block.sync
        def _(sp):
            sp.dma_start(cst[:, :], a["cst"]).then_inc(consts_in, 16)
            sp.dma_start(x[0:N_META, 0, :], a["meta_tokens"]).then_inc(x_in, 16)
            sp.dma_start(x[N_META:P, 0, :], a["x_prompt"][0, 0:P - N_META, :]).then_inc(x_in, 16)
            sp.dma_start(x[:, 1, :], a["x_prompt"][0, P - N_META:2 * P - N_META, :]).then_inc(x_in, 16)
            sp.wait_ge(x_zeroed, 1)
            sp.dma_start(x[0:TAIL, 2, :], a["x_prompt"][0, 2 * P - N_META:SEQ, :]).then_inc(x_in, 16)
            sp.dma_start(x[SAMPLE_ROW:SAMPLE_ROW + N_DEC, 2, :], a["x_sample"][0]).then_inc(x_in, 16)
            w = a["w_in0"].rearrange("(p k) n -> p k n", k=8)
            for i, (dst, c0, c1) in enumerate(((w_qk, 0, 512), (w_ac, C_A, D_IN), (w_v, C_V, C_R), (w_r, C_R, C_A))):
                sp.dma_start(dst, w[:, :, c0:c1]).then_inc(w_in[i], 16)
            banks.full(sp, ("att", TILES - 1, GH - 1))
            sp.dma_start(w_out, a["w_out0"].rearrange("(k p) n -> p k n", p=P)).then_inc(w_out_in, 16)
            sp.wait_ge(og_ready, TILES)
            load_shared(sp, 0)
            sp.wait_ge(x_ready, 3)
            sp.wait_ge(stored, 16 * MIX_STORES)
            sp_experts(sp, 0)
            sp_experts(sp, 1)
            sp.wait_ge(x_ready, 10)
            sp.dma_start(out["y_prompt"][0, 0:P - N_META, :], x[N_META:P, 0, :]).then_inc(y_stored, 16)
            sp.wait_ge(x_ready, 11)
            sp.dma_start(out["y_prompt"][0, P - N_META:2 * P - N_META, :], x[:, 1, :]).then_inc(y_stored, 16)
            sp.wait_ge(x_ready, 12)
            sp.dma_start(out["y_prompt"][0, 2 * P - N_META:SEQ, :], x[0:TAIL, 2, :]).then_inc(y_stored, 16)
            sp.dma_start(out["y_sample"][0], x[SAMPLE_ROW:SAMPLE_ROW + N_DEC, 2, :]).then_inc(y_stored, 16)
            sp.wait_ge(y_stored, 16 * 4)
            sp.wait_ge(stored, 16 * (MIX_STORES + 2))

        @block.gpsimd
        def _(gp):
            gp.memset(x[:, 2, :], 0.0).then_inc(x_zeroed, 1)
            gp.memset(xt[:, :, T_COLS:], 0.0).then_inc(L[0]["init"], 1)
            gp.dma_start(bg[:, :], a["gla_b_g"].rearrange("(j p) -> p j", p=P), allow_slow_non_contiguous=True).then_inc(mixp_in, 16)
            gp.dma_start(wg2[:, :], a["gla_w_g2"]).then_inc(mixp_in, 16)
            gp.dma_start(mix[:, :], a["mix"]).then_inc(mix_in, 16)
            gp.dma_start(g_q[:, :], a["mla_q_norm_g"].partition_broadcast(P)).then_inc(mixp_in, 16)
            gp.dma_start(g_kv[:, :], a["mla_kv_norm_g"].partition_broadcast(P)).then_inc(mixp_in, 16)
            gp.dma_start(g_gla[:, :], a["gla_norm_g"].partition_broadcast(P)).then_inc(mixp_in, 16)
            for k in range(2):
                uq = a["mla_w_uq"][k * P:(k + 1) * P, :].rearrange("p (h n) -> p h n", h=MH)
                gp.dma_start(w_uqn[:, k, :, :], uq[:, :, 0:NOPE]).then_inc(mixp_in, 16)
                gp.dma_start(w_uqr[:, k, :, :], uq[:, :, NOPE:]).then_inc(mixp_in, 16)
            gp.dma_start(w_uk[:, :], a["mla_w_uk"].rearrange("c h n -> c (h n)")).then_inc(mixp_in, 16)
            gp.dma_start(w_uv[:, :, :], a["mla_w_uv"]).then_inc(mixp_in, 16)
            for l in range(DEPTH):
                gp.dma_start(rbias[:, l, :], a["moe_router_b"][l].partition_broadcast(P)).then_inc(rbias_in, 16)
            ck, ckr = a["cache_mla_ckv"][0], a["cache_mla_krope"][0]
            for src, dst in ((ck, past), (ckr, past_r)):
                gp.memset(dst[:, 2, :], 0.0).then_inc(zeroed, 1)
            gp.wait_ge(zeroed, 2)
            for src, dst in ((ck, past), (ckr, past_r)):
                gp.dma_start(dst[:, 0:2, :], src[0:2 * P, :].rearrange("(t p) c -> p t c", p=P)).then_inc(past_in, 16)
                gp.dma_start(dst[0:TAIL, 2, :], src[2 * P:N_KEYS_PAST, :]).then_inc(past_in, 16)
            for t in (og[:, 2, :], kd_t[:, :, :], s_p[:, :, :], s_s[:, :, :], skv_t[:, :], skr_t[:, :],
                      qe_t[:, :, :], eps[:, 0:1]):
                gp.memset(t, LN_EPS if t.shape[-1] == 1 else 0.0).then_inc(zeroed, 1)
            gp.memset(eps[:, 1:2], RMS_EPS).then_inc(zeroed, 1)
            gp.memset(msq[:, :, :], 1.0).then_inc(zeroed, 1)
            gp.memset(gss[:, :], 1.0).then_inc(zeroed, 1)
            gp.wait_ge(zeroed, ZEROED)
            for h in range(GH):
                j, b = divmod(h, 2)
                gp.dma_start(s_s[64 * b:64 * b + 64, j, 128 * b:128 * b + 128], a["state_gla"][0, h]).then_inc(state_in, 16)
            banks.full(gp, ("c", TILES - 1))
            gp.memset(w_lo[:, 0:2 * half], 0.0).then_inc(levels_zeroed, 1)

            def load_ln(l, i):
                gp.dma_start(ln_g[:, :], a["ln_g"][l, i].partition_broadcast(P)).then_inc(ln_in, 16)
                gp.dma_start(ln_b[:, :], a["ln_b"][l, i].partition_broadcast(P)).then_inc(ln_in, 16)

            load_ln(0, 0)
            gp.wait_ge(c_normed, 3)
            for name, src in (("ckv", ckv_n), ("krope", kr)):
                po, so = out[f"prompt_{name}"][0], out[f"sample_{name}"][0]
                gp.dma_start(po[0:2 * P, :].rearrange("(t p) c -> p t c", p=P), src[:, 0:2, :]).then_inc(stored, 16)
                gp.dma_start(po[2 * P:N_PROMPT, :], src[0:TAIL, 2, :]).then_inc(stored, 16)
                gp.dma_start(so, src[SAMPLE_ROW:SAMPLE_ROW + N_DEC, 2, :]).then_inc(stored, 16)
            for j in range(2):
                banks.copied(gp, ("u", 4, j))
                banks.copied(gp, ("u", 5, j))
            for st, o in ((s_p, out["prompt_gla_state"]), (s_s, out["sample_gla_state"])):
                for h in range(GH):
                    j, b = divmod(h, 2)
                    gp.dma_start(o[0, h], st[64 * b:64 * b + 64, j, 128 * b:128 * b + 128]).then_inc(stored, 16)
            for l in range(DEPTH):
                s = L[l]
                if l:
                    gp.wait_ge(var_ready, 4)
                    gp.memset(pool_c, 0.0).then_inc(s["init"], 1)
                    gp.wait_ge(s["init"], 1)
                    gp.dma_start(pool_c[0:15, :], a["cache_pool"][0]).then_inc(s["pool_c_in"], 16)
                    gp.memset(xt[:, :, T_COLS:], 0.0).then_inc(s["init"], 1)
                    gp.wait_ge(x_ready, 6)
                    gp.dma_start(out["prompt_pool_rows"][0], x[TAIL - 15:TAIL, 2, :]).then_inc(stored, 16)
                    e = SAMPLE_ROW + N_DEC
                    gp.dma_start(out["sample_pool_rows"][0], x[e - 15:e, 2, :]).then_inc(stored, 16)
                    load_ln(1, 0)
                else:
                    gp.wait_ge(x_ready, 3)
                    gp.wait_ge(stored, 16 * MIX_STORES)
                for t in (place[1][:, :], place[0][:, T_COLS:], yh[:, :], yl[:, :]):
                    gp.memset(t.bitcast(F32), 0.0).then_inc(s["init"], 1)
                gp.wait_ge(x_ready, 3 + 6 * l)
                load_ln(l, 1)

        ident = const("ident")

        def transpose(pe, dst, src):
            n = src.shape[0]
            return pe.transpose(dst, src, ident[0:n, 0:n])

        def pe_transpose_x(pe, n):
            for i in range(5):
                t, k0, nk = xt_part(i)
                rows = ROWS[t]
                if n:
                    pe.wait_ge(x_ready, 3 * (2 * n - 2) + t + 1)
                ps = banks.open(pe, ("xT", n, i))
                for k in range(nk):
                    last = transpose(pe, ps[:, k * rows:(k + 1) * rows], x[0:rows, t, k0 + k::8])
                last.then_inc(banks.fill_sem(("xT", n, i)), 1)

        def accumulate(pe, dst, pairs):
            for i, (lhs, rhs) in enumerate(pairs):
                last = pe.matmul(dst, lhs, rhs, start=i == 0, stop=i == len(pairs) - 1)
            return last

        def pe_experts(pe, l):
            s = L[l]
            gu_b, ht_b = banks.tile[0], banks.tile[1]
            xg_b, y_b, cb_b = banks.tile[2:4], banks.tile[4:6], banks.tile[6:8]
            banks.all_copied(pe, ("sd", l, TILES - 1, 1))

            def gather(b, u):
                for kk in range(4):
                    last = accumulate(pe, xg_b[kk // 2][:, (kk % 2) * 2 * P:(kk % 2 + 1) * 2 * P], [
                        (part[:, t, 4 * u + kk::8], pick[b][:, t, :])
                        for part, t in ((xh, 0), (xl, 0), (xh, 1), (xl, 1), (xh, 2))])
                    if kk % 2:
                        last.then_inc(s[f"xg_done{kk // 2}"], 1)

            def place_add(u, n, t):
                for c in range(2):
                    pe.wait_ge(s[f"added{c}"], n + t + 1)
                    for i, part in enumerate((yh, yl)):
                        last = pe.matmul(cb_b[c][:, :], place[u][:, t * P:(t + 1) * P],
                                         part[:, c * 512:(c + 1) * 512], start=i == 0, stop=i == 1)
                    last.then_inc(s[f"sum_done{c}"], 1)

            def down(u, c, k):
                for e in range(2):
                    last = pe.matmul(y_b[c][64 * e:64 * e + 64, :], ht[:, k, 64 * e:64 * e + 64],
                                     w_down[u][:, e, k * D + c * 512:k * D + (c + 1) * 512],
                                     start=k == 0, stop=k == 1)
                return last

            pe.wait_ge(s["rounds_ready"], 1)
            rounds = pe.value_load(n_rounds[0:1, 0:1], min_val=1, max_val=MAX_ROUNDS)
            pe.wait_ge(s["x_split"], 2)
            pe.wait_ge(s["init"], 5 + l)
            pe.wait_ge(s["pick_ready"], 1)
            for u in range(2):
                if u:
                    pe.wait_ge(s["xg_copied0"], 1)
                    pe.wait_ge(s["xg_copied1"], 1)
                gather(0, u)
            with pe.Fori(0, rounds) as r:
                with pe.Fori(0, GROUPS // 2) as j:
                    for b in range(2):
                        for u in range(2):
                            n = r * GROUPS + 2 * j + b
                            i = 2 * n + u
                            pe.wait_ge(s[f"gu_in{u}"], 32 * n + 32)
                            if u == 0:
                                pe.wait_ge(s["xg_copied0"], i + 2)
                                pe.wait_ge(s["xg_copied1"], i + 2)
                            pe.wait_ge(s["place_copied"], i + 1)
                            for k in range(DK_SLICES):
                                for e in range(2):
                                    sl = slice(u * P + 64 * e, u * P + 64 * e + 64)
                                    last = pe.matmul(gu_b[64 * e:64 * e + 64, :], xgt[b][:, k, sl],
                                                     w_gu[u][:, :, e, k * FE:(k + 1) * FE],
                                                     start=k == 0, stop=k == DK_SLICES - 1)
                            last.then_inc(s[f"gu_done{u}"], 1)
                            if u == 0:
                                pe.wait_ge(s["pick_ready"], n + 2)
                            else:
                                pe.wait_ge(s["xg_copied0"], i + 2)
                                pe.wait_ge(s["xg_copied1"], i + 2)
                            gather(1 - b, u)
                            pe.wait_ge(s["h_ready"], i + 2)
                            for k in range(2):
                                last = transpose(pe, ht_b[:, k * P:(k + 1) * P], hh[:, k::2])
                            last.then_inc(s["ht_done"], 1)
                            pu = slice(u * P, (u + 1) * P)
                            for t in range(TILES):
                                rows = ROWS[t]
                                transpose(pe, gu_b[:, t * P:t * P + rows], pick[b][0:rows, t, pu].bitcast(F32))
                            accumulate(pe, gu_b[:, T_COLS:T_COLS + 2], [
                                (pick[b][:, t, pu].bitcast(F32), wpick[:, b, t, 2 * u:2 * u + 2])
                                for t in range(TILES)]).then_inc(s["place_done"], 1)
                            pe.wait_ge(s["y_ready"], 2 * i + 1)
                            place_add(1 - u, 3 * i, 0)
                            pe.wait_ge(s["ht_copied"], i + 1)
                            pe.wait_ge(s[f"down_in{u}"], 16 * n + 16)
                            down(u, 0, 0)
                            down(u, 0, 1)
                            place_add(1 - u, 3 * i, 1)
                            down(u, 1, 0)
                            place_add(1 - u, 3 * i, 2)
                            down(u, 1, 1).then_inc(s[f"down_done{u}"], 1)
            total = rounds * PAIRS
            pe.wait_ge(s["y_ready"], 2 * total + 1)
            for t in range(TILES):
                place_add(1, 3 * total, t)

        @block.tensor
        def _(pe):
            for l in range(DEPTH):
                for n in ("added0", "added1", "place_copied", "y_ready", "h_ready", "place_done"):
                    pe.sem_inc(L[l][n], 1)
            pe.wait_ge(consts_in, 16)
            pe.wait_ge(x_in, 16 * 5)
            pe_transpose_x(pe, 0)

            def stage(name, pairs_of):
                ps = banks.open(pe, name)
                return pairs_of(ps).then_inc(banks.fill_sem(name), 1)

            def token_products(name, tag, lhs, w, nk):
                for t in range(TILES):
                    tc = slice(t * P, t * P + ROWS[t])
                    at = (name,) + ((tag,) if tag is not None else ()) + (t,)
                    if t < 2:
                        for c in range(2):
                            stage(at + (c,), lambda ps: accumulate(pe, ps[:, :], [
                                (lhs(k, tc), w[:, k, c * 512:(c + 1) * 512]) for k in range(nk)]))
                        continue
                    both = [banks.open(pe, at + (c,)) for c in range(2)]
                    for k in range(nk):
                        for c in range(2):
                            last = pe.matmul(both[c][64 * c:64 * c + 64, :], lhs(k, tc), w[:, k, c * 512:(c + 1) * 512],
                                             start=k == 0, stop=k == nk - 1)
                            if k == nk - 1:
                                last.then_inc(banks.fill_sem(at + (c,)), 1)

            for i in range(5):
                banks.copied(pe, ("xT", 0, i))
            pe.wait_ge(w_in[0], 16)
            for j in range(4):
                stage(("qk", j), lambda ps: accumulate(pe, ps[:, 0:T_COLS], [
                    (w_qk[:, k, j * P:(j + 1) * P], xt[:, k, 0:T_COLS]) for k in range(8)]))
            pe.wait_ge(w_in[1], 16)
            stage(("a",), lambda ps: accumulate(pe, ps[0:GRANK, 0:T_COLS], [
                (w_ac[:, k, 0:GRANK], xt[:, k, 0:T_COLS]) for k in range(8)]))
            banks.copied(pe, ("a",))
            pe.wait_ge(mixp_in, 16 * MIX_PARAMS)
            for j in range(2):
                stage(("z", j), lambda ps: pe.matmul(ps[:, 0:T_COLS], wg2[:, j * P:(j + 1) * P], a_t[:, :],
                                                     start=True, stop=True))
            for name, w, c0, n in (("c", w_ac, GRANK, 416), ("v", w_v, 0, 512)):
                if name != "c":
                    pe.wait_ge(w_in[2], 16)
                for t in range(TILES):
                    tc = slice(t * P, t * P + ROWS[t])
                    if t < 2:
                        stage((name, t), lambda ps: accumulate(pe, ps[:, 0:n], [
                            (xt[:, k, tc], w[:, k, c0:c0 + n]) for k in range(8)]))
                        continue
                    ps = banks.open(pe, (name, t))
                    for k in range(8):
                        for c in range(2):
                            last = pe.matmul(ps[64 * c:64 * c + 64, 0:n // 2], xt[:, k, tc],
                                             w[:, k, c0 + c * n // 2:c0 + (c + 1) * n // 2], start=k == 0, stop=k == 7)
                    last.then_inc(banks.fill_sem((name, t)), 1)
            pe.wait_ge(w_in[3], 16)
            for j in range(4):
                stage(("r", j), lambda ps: accumulate(pe, ps[:, 0:T_COLS], [
                    (w_r[:, k, j * P:(j + 1) * P], xt[:, k, 0:T_COLS]) for k in range(8)]))
            for t in range(TILES):
                rows = ROWS[t]
                pe.wait_ge(c_normed, t + 1)
                ps = banks.open(pe, ("mT", t))
                for k in range(2):
                    transpose(pe, ps[:, k * P:k * P + rows], cq_n[0:rows, t, k * P:(k + 1) * P])
                transpose(pe, ps[:, 256:256 + rows], ckv_n[0:rows, t, :])
                transpose(pe, ps[0:ROPE, 384:384 + rows], kr[0:rows, t, :]).then_inc(banks.fill_sem(("mT", t)), 1)
            pe.wait_ge(past_in, 16 * 4)
            for g in range(TILES):
                rows = P if g < 2 else TAIL
                ps = banks.open(pe, ("pT", g))
                transpose(pe, ps[:, 0:rows], past[0:rows, g, :])
                transpose(pe, ps[0:ROPE, P:P + rows], past_r[0:rows, g, :]).then_inc(banks.fill_sem(("pT", g)), 1)
            ps = banks.open(pe, ("ukT",))
            for g in range(4):
                last = transpose(pe, ps[:, g * P:(g + 1) * P], w_uk[:, g * P:(g + 1) * P])
            last.then_inc(banks.fill_sem(("ukT",)), 1)
            for t in range(TILES):
                banks.copied(pe, ("mT", t))
            for g in range(4):
                stage(("qn", g), lambda ps: accumulate(pe, ps[:, 0:T_COLS], [
                    (w_uqn[:, k, 2 * g:2 * g + 2, :].rearrange("p h n -> p (h n)"), cq_t[:, k, :]) for k in range(2)]))
            for t in range(TILES):
                rows = ROWS[t]
                stage(("qr", t), lambda ps: accumulate(pe, ps[0:rows, 0:256], [
                    (cq_t[:, k, t * P:t * P + rows], w_uqr[:, k, :, :].rearrange("p h n -> p (h n)")) for k in range(2)]))
            pe.wait_ge(qe_ready, 2)
            for t in range(TILES):
                rows = ROWS[t]
                ps = banks.open(pe, ("kd", t))
                for j in range(2):
                    last = transpose(pe, ps[0:rows, j * P:(j + 1) * P], kd_t[:, j, t * P:t * P + rows])
                last.then_inc(banks.fill_sem(("kd", t)), 1)
            pe.wait_ge(lev_ready, LEVELS)
            pe.wait_ge(zeroed, ZEROED)
            pe.wait_ge(state_in, 16 * GH)
            for t in range(TILES):
                banks.copied(pe, ("kd", t))

            def level_products(t):
                for h in range(GH):
                    j, hb = h // 2, 64 * (h % 2)
                    ps = banks.open(pe, ("att", t, h))
                    for v in range(LEVELS + 1):
                        for tt_, pb, n in CHUNKS:
                            if tt_ != t or v > int(math.log2(n)):
                                continue
                            c0 = t * P + pb
                            kk = k_t[hb:hb + 64, j, c0:c0 + n] if v == 0 else k_lev[hb:hb + 64, v - 1, j, c0:c0 + n]
                            qq = q_t[hb:hb + 64, j, c0:c0 + n] if v == 0 else q_lev[hb:hb + 64, v - 1, j, c0:c0 + n]
                            o0 = v * CHUNK + pb % CHUNK
                            last = pe.matmul(ps[pb:pb + n, o0:o0 + n], kk, qq, start=True, stop=True)
                    last.then_inc(banks.fill_sem(("att", t, h)), 1)

            def chunk_out(c):
                t, pb, n = CHUNKS[c]
                c0, o0 = t * P + pb, pb % CHUNK
                st = s_s if c == 5 else s_p
                if 0 < c < 5:
                    for j in range(2):
                        banks.copied(pe, ("u", c - 1, j))
                for j in range(2):
                    ps = banks.open(pe, ("o", c, j))
                    pe.matmul(ps[pb:pb + n, 0:256], qe_t[:, j, c0:c0 + n], st[:, j, :], start=True, stop=False)
                    for b in range(2):
                        h = 2 * j + b
                        pe.wait_ge(att_ready, 4 * t + h + 1)
                        last = pe.matmul(ps[pb:pb + n, b * P:(b + 1) * P], att[pb:pb + n, t, h, o0:o0 + n],
                                         v_sb[pb:pb + n, t, h * P:(h + 1) * P], start=False, stop=b == 1)
                    last.then_inc(banks.fill_sem(("o", c, j)), 1)
                    stage(("u", c, j), lambda ps: pe.matmul(ps[:, 0:256], kd[pb:pb + n, t, j * P:(j + 1) * P],
                                                            v_sb[pb:pb + n, t, j * 256:(j + 1) * 256],
                                                            start=True, stop=True))

            def absorbed_queries():
                for h in range(MH):
                    g, hb = h // 2, 64 * (h % 2)
                    stage(("ql", h), lambda ps: pe.matmul(ps[:, 0:T_COLS], uk_t[hb:hb + 64, g, :], q_n_t[hb:hb + 64, g, :],
                                                          start=True, stop=True))

            def rotated_queries():
                pe.wait_ge(qrot_ready, TILES)
                for i in range(5):
                    t, h0, nh = xt_part(i)
                    rows = ROWS[t]
                    ps = banks.open(pe, ("qrT", i))
                    for h in range(nh):
                        last = transpose(pe, ps[0:ROPE, h * rows:(h + 1) * rows],
                                         q_rot[0:rows, t, (h0 + h) * ROPE:(h0 + h + 1) * ROPE])
                    last.then_inc(banks.fill_sem(("qrT", i)), 1)

            for g in range(4):
                banks.copied(pe, ("qn", g))
            banks.copied(pe, ("ukT",))
            for t in range(TILES):
                level_products(t)
                if t < 2:
                    (absorbed_queries, rotated_queries)[t]()
                for c in CHUNKS_BY_TILE[t]:
                    chunk_out(c)
            blocks = attention_blocks()
            for h in range(MH):
                banks.copied(pe, ("ql", h))
            for i in range(5):
                banks.copied(pe, ("qrT", i))
            pe.wait_ge(skeys_ready, 2)
            for i in range(len(blocks) + 3):
                if i < len(blocks):
                    hs, q0, nq, nk, _, sample = blocks[i]
                    kt, krt = (skv_t, skr_t) if sample else (kv_t, kr_t)
                    if len(hs) == 1:
                        ql, qr = q_lat[:, hs[0], q0:q0 + nq], q_rot_t[0:ROPE, hs[0], q0:q0 + nq]
                    else:
                        c0 = MH * TAIL + hs[0] * N_DEC if sample else 0
                        ql, qr = q_few[:, c0:c0 + P], q_few_rot[:, c0:c0 + P]
                    stage(("s", i), lambda ps: accumulate(pe, ps[:, 0:nk], [
                        (ql, kt[:, 0:nk]),
                        (qr, krt[:, 0:nk])]))
                key_tiles = lambda m: [(k, min(P, blocks[m][3] - k * P)) for k in range(-(-blocks[m][3] // P))]
                m = i - 2
                if 0 <= m < len(blocks):
                    pe.wait_ge(p_ready, m + 1)
                    ps = banks.open(pe, ("pt", m))
                    for k, rows in key_tiles(m):
                        last = transpose(pe, ps[0:rows, k * P:(k + 1) * P], sm[:, m % 4, k * P:k * P + rows])
                    last.then_inc(banks.fill_sem(("pt", m)), 1)
                m = i - 3
                if m >= 0:
                    banks.copied(pe, ("pt", m))
                    src = past if blocks[m][5] else ckv_n
                    stage(("ol", m), lambda ps: accumulate(pe, ps[:, 0:P], [
                        (src[0:rows, k, :], p_t[0:rows, m % 2, k, :]) for k, rows in key_tiles(m)]))
            pe.wait_ge(og_ready, TILES)
            for t in range(TILES):
                rows = ROWS[t]
                ps = banks.open(pe, ("ogT", t))
                for h in range(GH):
                    last = transpose(pe, ps[:, h * rows:(h + 1) * rows], og[0:rows, t, h * P:(h + 1) * P])
                last.then_inc(banks.fill_sem(("ogT", t)), 1)
            for m in range(len(blocks)):
                banks.copied(pe, ("ol", m))
            for g in range(4):
                ps = banks.open(pe, ("om", g))
                for b in range(2):
                    last = pe.matmul(ps[64 * b:64 * b + 64, 0:T_COLS], w_uv[:, 2 * g + b, :], q_lat[:, 2 * g + b, :],
                                     start=True, stop=True)
                last.then_inc(banks.fill_sem(("om", g)), 1)
            for t in range(TILES):
                banks.copied(pe, ("ogT", t))
            for g in range(4):
                banks.copied(pe, ("om", g))
            pe.wait_ge(w_out_in, 16)
            token_products("mo", None, lambda k, tc: o_t[:, k, tc], w_out, 8)
            for l in range(DEPTH):
                s = L[l]
                if l:
                    pe.wait_ge(s["pool_in"], 16 * 3)
                    bd = {n: band[:, slice(*BAND[n])].rearrange("p (g t) -> p g t", g=4) for n in BAND}
                    mixed = [banks.open(pe, ("mx", c)) for c in range(DK_SLICES)]
                    for t in range(TILES):
                        pe.wait_ge(x_ready, 3 + t + 1)
                        if t == TILES - 1:
                            pe.wait_ge(s["pool_c_in"], 16)
                        for c, ps in enumerate(mixed):
                            g, cc = c // 2, slice(c * P, (c + 1) * P)
                            last = accumulate(pe, ps[:, t * P:t * P + ROWS[t]], (
                                [(x[:, 0, cc], bd["own0"][:, g, :])],
                                [(x[:, 0, cc], bd["prev1"][:, g, :]), (x[:, 1, cc], bd["own1"][:, g, :])],
                                [(x[:, 1, cc], bd["prev2"][:, g, :]), (x[0:64, 2, cc], bd["own2"][0:64, g, :]),
                                 (pool_c[0:64, cc], bd["cache"][0:64, g, :])])[t])
                            if t == TILES - 1:
                                last.then_inc(banks.fill_sem(("mx", c)), 1)
                    for c in range(DK_SLICES):
                        banks.copied(pe, ("mx", c))
                    for t in range(TILES):
                        rows = ROWS[t]
                        for c in range(2):
                            ps = banks.open(pe, ("po", t, c))
                            for g in range(2):
                                last = accumulate(pe, ps[0:rows, g * PG:(g + 1) * PG], [
                                    (xt[:, 4 * c + 2 * g + k, t * P:t * P + rows], pool_w[:, 2 * c + g, k, :]) for k in range(2)])
                            last.then_inc(banks.fill_sem(("po", t, c)), 1)
                pe_transpose_x(pe, l + 1)
                for i in range(5):
                    banks.copied(pe, ("xT", l + 1, i))
                pe.wait_ge(s["init"], 1 + l)
                pe.wait_ge(s["router_in"], 16)
                ps = banks.open(pe, ("lg", l))
                for t in range(TILES):
                    last = accumulate(pe, ps[:, t * E:(t + 1) * E], [(xt[:, k, t * P:(t + 1) * P], w_rt[:, k, :]) for k in range(8)])
                last.then_inc(banks.fill_sem(("lg", l)), 1)
                pe.wait_ge(s["shared_in"], 16 * 3)
                for b in range(2):
                    for name, w in (("sg", sh_gate), ("su", sh_up)):
                        stage((name, l, b), lambda ps: accumulate(pe, ps[:, 0:T_COLS], [
                            (w[:, k, b::2], xt[:, k, 0:T_COLS]) for k in range(8)]))
                pe.wait_ge(s["sel_ready"], 1)
                ps = banks.open(pe, ("pos", l))
                for t in range(TILES):
                    accumulate(pe, ps[:, t * E:(t + 1) * E], [(const("ones"), sel[:, i, :]) for i in range(t)] +
                               [(const("before"), sel[:, t, :])])
                accumulate(pe, ps[:, TILES * E:(TILES + 1) * E], [(const("ones"), sel[:, i, :]) for i in range(TILES)])\
                    .then_inc(banks.fill_sem(("pos", l)), 1)
                for b in range(2):
                    banks.copied(pe, ("su", l, b))
                token_products("sd", l, lambda k, tc: sh_h[:, k, tc], sh_down, 2)
                pe_experts(pe, l)

        def act_experts(act, l):
            s = L[l]
            gu_b, ht_b = banks.tile[0], banks.tile[1]
            act.wait_ge(s["rounds_ready"], 1)
            rounds = act.value_load(n_rounds[0:1, 0:1], min_val=1, max_val=MAX_ROUNDS)

            def copy_xg(b, u, n):
                act.wait_ge(s["xg_done0"], n)
                act.activation(xgt[b][:, 4 * u:4 * u + 2, :], banks.tile[2][:, :].rearrange("p (k n) -> p k n", k=2), ACT.Copy)\
                   .then_inc(s["xg_copied0"], 1)

            for u in range(2):
                copy_xg(0, u, u + 1)
            with act.Fori(0, rounds) as r:
                with act.Fori(0, GROUPS // 2) as j:
                    for b in range(2):
                        for u in range(2):
                            n = r * GROUPS + 2 * j + b
                            i = 2 * n + u
                            act.wait_ge(s[f"gu_done{u}"], n + 1)
                            act.wait_ge(s["h_ready"], i + 1)
                            act.activation(sg[:, :], gu_b[:, 0:FE], ACT.Silu).then_inc(s["sg_ready"], 1)
                            copy_xg(1 - b, u, i + 3)
                            act.wait_ge(s["ht_done"], i + 1)
                            act.activation(ht[:, :, :], ht_b[:, 0:2 * P].rearrange("p (k n) -> p k n", k=2), ACT.Copy)\
                               .then_inc(s["ht_copied"], 1)
                            act.wait_ge(s["place_done"], i + 2)
                            for e in range(2):
                                act.activation(gslot[64 * e:64 * e + 64, u, :],
                                               gu_b[64 * e:64 * e + 64, T_COLS + e:T_COLS + e + 1], ACT.Copy)\
                                   .then_inc(act_gate[l], 1)
                            act.activation(place[u][:, 0:T_COLS], gu_b[:, 0:T_COLS], ACT.Copy).then_inc(s["place_copied"], 1)
                            act.wait_ge(s[f"down_done{u}"], n + 1)
                            act.wait_ge(act_gate[l], 2 * i + 2)
                            for c in range(2):
                                act.activation(yh[:, c * 512:(c + 1) * 512], banks.tile[4 + c][:, :], ACT.Copy,
                                               scale=gslot[:, u, :]).then_inc(s[f"yh_ready{c}"], 1)

        @block.scalar
        def _(act):
            step = Steps(act, act_step)

            def copy(dst, name, src=None):
                ps = banks.full(act, name)
                act.activation(dst, src(ps) if src else ps, ACT.Copy).then_inc(banks.empty_sem(name), 1)

            def copy_xt(n):
                for i in range(0, 5, 2):
                    t, k0, nk = xt_part(i)
                    copy(xt_in_cols(i), ("xT", n, i), lambda ps: ps[:, 0:nk * ROWS[t]].rearrange("p (k n) -> p k n", k=nk))

            def rsqrt(dst, src, scale, bias, sem=None):
                step(act.activation(dst, src, ACT.Ln, scale=scale, bias=bias))
                step(act.activation(dst, dst, ACT.Exp, scale=-0.5), sem)

            def ln_rsqrt(n):
                for t in range(TILES):
                    rows = ROWS[t]
                    act.wait_ge(var_ready, 3 * n + t + 1)
                    rsqrt(ln_rs[0:rows, t:t + 1], ln_mv[0:rows, t, 1:2], 1.0, eps[0:rows, 0:1], rs_ready)

            copy_xt(0)
            for j in range(2, 4):
                copy(k_t[:, j - 2, :], ("qk", j), lambda ps: ps[:, 0:T_COLS])
            copy(a_t[:, :], ("a",), lambda ps: ps[0:GRANK, 0:T_COLS])
            act.wait_ge(z_ready, 2)
            step(act.activation(u_t[:, :, :], z_t[:, :, :], ACT.Abs))
            step(act.activation(u_t[:, :, :], u_t[:, :, :], ACT.Exp, scale=-1.0))
            step(act.activation(u_t[:, :, :], u_t[:, :, :], ACT.Ln, bias=1.0), ls_ready)
            act.wait_ge(zeroed, ZEROED)
            for t in range(TILES):
                rows = ROWS[t]
                banks.copied(act, ("c", t))
                step(act.activation(sq[0:rows, 0:QL_R], c_sb[0:rows, t, 0:QL_R], ACT.Square, accum_out=msq[0:rows, 0, t:t + 1]))
                step(act.activation(sq[0:rows, 0:KVL], c_sb[0:rows, t, QL_R:QL_R + KVL], ACT.Square, accum_out=msq[0:rows, 1, t:t + 1]))
            rsqrt(mrs[:, 0, 0:3], msq[:, 0, 0:3], 1.0 / QL_R, eps[:, 1:2], c_sq)
            rsqrt(mrs[:, 1, 0:3], msq[:, 1, 0:3], 1.0 / KVL, eps[:, 1:2], c_sq)
            act.wait_ge(b_ready, 1)
            step(act.activation(u_t[:, :, :], b_t[:, :, :], ACT.Exp), eb_ready)
            act.wait_ge(dk_ready, 1)
            step(act.activation(kd_t[:, :, :], kd_t[:, :, :], ACT.Exp), ek_ready)
            for t in range(2):
                copy(v_sb[:, t, :], ("v", t), lambda ps: ps[:, :])
            ps = banks.full(act, ("v", 2))
            act.activation(v_sb[0:64, 2, 0:256], ps[0:64, 0:256], ACT.Copy)
            act.activation(v_sb[0:64, 2, 256:512], ps[64:128, 0:256], ACT.Copy).then_inc(banks.empty_sem(("v", 2)), 1)
            for v in range(LEVELS):
                act.wait_ge(lev_d, v + 1)
                for w, part in ((q_lev, 1), (k_lev, 0)):
                    for j in range(2):
                        ap = level_half(w[:, v, j, :], v, part)
                        ins = act.activation(ap, ap, ACT.Exp)
                        if part == 0 and j == 1:
                            step(ins, lev_e)
            for j in range(4):
                ps = banks.full(act, ("r", j))
                act.activation(r_t[:, j, :], ps[:, 0:T_COLS], ACT.Silu).then_inc(banks.empty_sem(("r", j)), 1)
            for t in range(TILES):
                rows, n = ROWS[t], ("mT", t)
                cols = slice(t * P, t * P + rows)
                ps = banks.full(act, n)
                act.activation(cq_t[:, :, cols], ps[:, 0:256].rearrange("p (k n) -> p k n", k=2)[:, :, 0:rows], ACT.Copy)
                act.activation(kv_t[:, cols], ps[:, 256:256 + rows], ACT.Copy)
                act.activation(kr_t[:, cols], ps[0:ROPE, 384:384 + rows], ACT.Copy).then_inc(banks.empty_sem(n), 1)
            for g in range(TILES):
                rows, n = P if g < 2 else TAIL, ("pT", g)
                ps = banks.full(act, n)
                act.activation(skv_t[:, g * P:g * P + rows], ps[:, 0:rows], ACT.Copy)
                act.activation(skr_t[:, g * P:g * P + rows], ps[0:ROPE, P:P + rows], ACT.Copy).then_inc(banks.empty_sem(n), 1)
            copy(uk_t[:, :, :], ("ukT",), lambda ps: ps[:, :].rearrange("p (g n) -> p g n", g=4))
            for g in range(4):
                copy(q_n_t[:, g, :], ("qn", g), lambda ps: ps[:, 0:T_COLS])
            for t in range(TILES):
                rows = ROWS[t]
                copy(kd[0:rows, t, :], ("kd", t), lambda ps: ps[0:rows, 0:256])
            banks.copied(act, ("mT", 2))
            own = slice(SAMPLE_ROW, SAMPLE_ROW + N_DEC)
            act.wait_ge(past_in, 16 * 4)
            act.wait_ge(c_normed, 3)
            act.activation(skv_t[:, SAMPLE0:], kv_t[:, SAMPLE0:], ACT.Copy)
            act.activation(skr_t[:, SAMPLE0:], kr_t[:, SAMPLE0:], ACT.Copy)
            act.activation(past[own, 2, :], ckv_n[own, 2, :], ACT.Copy).then_inc(skeys_ready, 1)
            act.wait_ge(zeroed, ZEROED)
            for t in range(TILES):
                if t == 0:
                    for h in range(MH):
                        copy(q_lat[:, h, :], ("ql", h), lambda ps: ps[:, 0:T_COLS])
                if t == 1:
                    for i in range(5):
                        tq, h0, nh = xt_part(i)
                        rows = ROWS[tq]
                        copy(q_rot_t[0:ROPE, h0:h0 + nh, tq * P:tq * P + rows], ("qrT", i),
                             lambda ps: ps[0:ROPE, 0:nh * rows].rearrange("p (h n) -> p h n", h=nh))
                for c in CHUNKS_BY_TILE[t]:
                    tc, pb, n = CHUNKS[c]
                    for j in range(2):
                        copy(og[pb:pb + n, tc, j * 256:(j + 1) * 256], ("o", c, j), lambda ps: ps[pb:pb + n, 0:256])
            for h in range(MH):
                banks.copied(act, ("ql", h))
            for i in range(5):
                banks.copied(act, ("qrT", i))
            for src, dst in ((q_lat, q_few), (q_rot_t[0:ROPE, :, :], q_few_rot)):
                for c0, q0, nq in ((0, 2 * P, TAIL), (MH * TAIL, SAMPLE0, N_DEC)):
                    ins = act.activation(dst[:, c0:c0 + MH * nq].rearrange("p (h t) -> p h t", h=MH), src[:, :, q0:q0 + nq], ACT.Copy)
            ins.then_inc(skeys_ready, 1)
            act.wait_ge(gss_ready, TILES)
            rsqrt(grs[:, :], gss[:, :], 1.0 / GDV, eps[:, 1:2], grs_ready)
            blocks = attention_blocks()

            def exp_block(m):
                nk = blocks[m][3]
                act.wait_ge(mx_ready, m + 1)
                act.activation(sm[:, m % 4, 0:nk], sm[:, m % 4, 0:nk], ACT.Exp, bias=stat[:, m % 4, 1:2],
                               accum_out=stat[:, m % 4, 2:3]).then_inc(ex_ready, 1)

            exp_block(0)
            for m in range(len(blocks)):
                if m + 1 < len(blocks):
                    exp_block(m + 1)
                nk = blocks[m][3]
                ps = banks.full(act, ("pt", m))
                full, rest = divmod(nk, P)
                act.activation(p_t[:, m % 2, 0:full, :], ps[:, 0:full * P].rearrange("p (k n) -> p k n", k=full), ACT.Copy)
                act.activation(p_t[0:rest, m % 2, full, :], ps[0:rest, full * P:(full + 1) * P], ACT.Copy)\
                   .then_inc(banks.empty_sem(("pt", m)), 1)
            ln_rsqrt(0)
            for l in range(DEPTH):
                s = L[l]
                if l:
                    for c in range(0, DK_SLICES, 2):
                        copy(xt[:, c, 0:T_COLS], ("mx", c), lambda ps: ps[:, 0:T_COLS])
                    ln_rsqrt(2)
                copy_xt(l + 1)
                if l == 0:
                    act.wait_ge(stored, 16 * MIX_STORES)
                act.wait_ge(x_ready, 3 + 6 * l)
                ps = banks.full(act, ("lg", l))
                act.activation(sc[:, :, :], ps[:, 0:TILES * E].rearrange("p (t e) -> p t e", t=TILES), ACT.Exp, scale=-1.0)\
                   .then_inc(banks.empty_sem(("lg", l)), 1)
                act.activation(xh[:, 0:2, :], x[:, 0:2, :], ACT.Copy)
                act.activation(xh[0:64, 2, :], x[0:64, 2, :], ACT.Copy).then_inc(s["x_split"], 1)
                for b in range(2):
                    ins = act.activation(sh_sg[:, b, :], banks.full(act, ("sg", l, b))[:, 0:T_COLS], ACT.Silu)
                    ins.then_inc(banks.empty_sem(("sg", l, b)), 1)
                for t in range(TILES):
                    rows = ROWS[t]
                    copy(acc[0:rows, t, 0:512], ("sd", l, t, 0), lambda ps: ps[0:rows, :])
                act_experts(act, l)
                ln_rsqrt(2 * l + 1)

        def dve_experts(dve, l, step):
            s = L[l]
            gu_b = banks.tile[0]
            rounds = dve.value_load(n_rounds[0:1, 0:1], min_val=1, max_val=MAX_ROUNDS)
            iota = bc(bc(const("iota"), 1, 4), 1, TILES)

            def pick_group(b, c0):
                dve.tensor_copy(wpick[:, b, :, :], wt_x[:, :, c0])
                dve.tensor_tensor(pick[b][:, :, :].rearrange("p t (e n) -> p t e n", e=4), iota,
                                  bc(pos_x[:, :, c0], 3, SLOTS), ALU.is_equal).then_inc(s["pick_ready"], 1)

            def copy_xg(b, u, n):
                dve.wait_ge(s["xg_done1"], n)
                dve.tensor_copy(xgt[b][:, 4 * u + 2:4 * u + 4, :], banks.tile[3][:, :].rearrange("p (k n) -> p k n", k=2))\
                   .then_inc(s["xg_copied1"], 1)

            def add_sums(n):
                for t in range(TILES):
                    rows = ROWS[t]
                    for c in range(2):
                        dst = acc[0:rows, t, c * 512:(c + 1) * 512]
                        dve.wait_ge(s[f"sum_done{c}"], n + t + 1)
                        dve.tensor_tensor(dst, dst, banks.tile[6 + c][0:rows, :], ALU.add).then_inc(s[f"added{c}"], 1)

            pick_group(0, slice(0, 4))
            for u in range(2):
                copy_xg(0, u, u + 1)
            banks.copied(dve, ("sd", l, TILES - 1, 0))
            banks.copied(dve, ("sd", l, TILES - 1, 1))
            with dve.Fori(0, rounds) as r:
                with dve.Fori(0, GROUPS // 2) as j:
                    for b in range(2):
                        for u in range(2):
                            n = r * GROUPS + 2 * j + b
                            i = 2 * n + u
                            if u == 0:
                                dve.wait_ge(s["place_done"], i + 1)
                                pick_group(1 - b, bass.ds(8 * j + 4 * b + 4, 4))
                            dve.wait_ge(s["sg_ready"], i + 1)
                            dve.tensor_tensor(hh[:, :], sg[:, :], gu_b[:, FE:2 * FE], ALU.mult).then_inc(s["h_ready"], 1)
                            copy_xg(1 - b, u, i + 3)
                            add_sums(3 * i)
                            for c in range(2):
                                dve.wait_ge(s[f"yh_ready{c}"], i + 1)
                                cc = slice(c * 512, (c + 1) * 512)
                                dve.scalar_tensor_tensor(out=yl[:, cc], in0=banks.tile[4 + c][:, :], scalar=gslot[:, u, :],
                                                         in1=yh[:, cc].bitcast(F32), op0=ALU.mult, op1=ALU.subtract)\
                                   .then_inc(s["y_ready"], 1)
                dve.tensor_scalar(pos_x[:, :, :], pos_x[:, :, :], -float(SLOTS), None, ALU.add).then_inc(s["next_round"], 1)
                dve.wait_ge(s["next_round"], r + 1)
            add_sums(3 * PAIRS * rounds)

        @block.vector
        def _(dve):
            step = Steps(dve, dve_step)

            def tt(dst, x0, x1, op, sem=None):
                step(dve.tensor_tensor(dst, x0, x1, op), sem)

            def ts(dst, x0, s1, s2, o1, o2=None, sem=None):
                step(dve.tensor_scalar(dst, x0, s1, s2, o1, o2) if o2 is not None else dve.tensor_scalar(dst, x0, s1, s2, o1), sem)

            def copy(dst, name, src):
                ps = banks.full(dve, name)
                dve.tensor_copy(dst, src(ps)).then_inc(banks.empty_sem(name), 1)

            def copy_xt(n):
                for i in range(1, 5, 2):
                    t, k0, nk = xt_part(i)
                    copy(xt_in_cols(i), ("xT", n, i), lambda ps: ps[:, 0:nk * ROWS[t]].rearrange("p (k n) -> p k n", k=nk))

            def layer_norm(n, before):
                for t in range(TILES + 1):
                    if t < TILES:
                        rows = ROWS[t]
                        before(t, rows)
                        for c in range(2):
                            step(dve.bn_stats(ln_st[0:rows, t, c, :], x[0:rows, t, c * 512:(c + 1) * 512]))
                        step(dve.bn_aggr(ln_mv[0:rows, t, :], ln_st[0:rows, t, :, :].rearrange("p a b -> p (a b)")), var_ready)
                    if t == 0:
                        dve.wait_ge(ln_in, 32 * (n + 1))
                    else:
                        rows = ROWS[t - 1]
                        xr = x[0:rows, t - 1, :]
                        step(dve.scalar_tensor_tensor(out=xr, in0=xr, scalar=ln_mv[0:rows, t - 1, 0:1], in1=ln_g[0:rows, :],
                                                      op0=ALU.subtract, op1=ALU.mult))
                        dve.wait_ge(rs_ready, 3 * n + t)
                        step(dve.scalar_tensor_tensor(out=xr, in0=xr, scalar=ln_rs[0:rows, t - 1:t], in1=ln_b[0:rows, :],
                                                      op0=ALU.mult, op1=ALU.add), x_ready)

            copy_xt(0)
            for j in range(2):
                ps = banks.full(dve, ("qk", j))
                dve.tensor_scalar(q_t[:, j, :], ps[:, 0:T_COLS], GDK ** -0.5, None, ALU.mult).then_inc(banks.empty_sem(("qk", j)), 1)
            dve.wait_ge(mixp_in, 16 * MIX_PARAMS)
            for j in range(2):
                ps = banks.full(dve, ("z", j))
                step.banked(dve.tensor_scalar(z_t[:, j, :], ps[:, 0:T_COLS], bg[:, j:j + 1], None, ALU.add), banks, ("z", j))
            step(dve.tensor_copy(stat[:, 0, 0:2], bg[:, 0:2]), z_ready)
            step(dve.tensor_copy(stat[:, 0, 0:2], bg[:, 0:2]), z_ready)
            for t in range(2):
                copy(c_sb[:, t, :], ("c", t), lambda ps: ps[:, 0:416])
            ps = banks.full(dve, ("c", 2))
            dve.tensor_copy(c_sb[0:64, 2, 0:208], ps[0:64, 0:208])
            dve.tensor_copy(c_sb[0:64, 2, 208:416], ps[64:128, 0:208]).then_inc(banks.empty_sem(("c", 2)), 1)
            dve.wait_ge(ls_ready, 1)
            for j in range(2):
                step(dve.scalar_tensor_tensor(out=z_t[:, j, :], in0=z_t[:, j, :], scalar=0.0, in1=u_t[:, j, :],
                                              op0=ALU.min, op1=ALU.subtract))
            ts(z_t[:, :, :], z_t[:, :, :], 1.0 / TAU, None, ALU.mult)
            dve.wait_ge(mix_in, 16)
            reset = mixc("scan")
            for j in range(2):
                step(dve.tensor_tensor_scan(b_t[:, j, :], reset, z_t[:, j, :], 0.0, ALU.mult, ALU.add),
                     b_ready if j else None)
            dve.wait_ge(zeroed, ZEROED)
            bm = b_t[:, :, 0:256].rearrange("p j (c t) -> p j c t", t=CHUNK)
            tt(kd_t[:, :, 0:256].rearrange("p j (c t) -> p j c t", t=CHUNK), bc(bm[:, :, :, CHUNK - 1], 3, CHUNK), bm, ALU.subtract)
            for c0, n in ((2 * P, TAIL), (SAMPLE0, N_DEC)):
                tt(kd_t[:, :, c0:c0 + n], bc(b_t[:, :, c0 + n - 1], 2, n), b_t[:, :, c0:c0 + n], ALU.subtract,
                   dk_ready if n == N_DEC else None)
            dve.wait_ge(eb_ready, 1)
            tt(qe_t[:, :, :], q_t[:, :, :], u_t[:, :, :], ALU.mult, qe_ready)
            dve.wait_ge(ek_ready, 1)
            for j in range(2, 4):
                banks.copied(dve, ("qk", j))
            tt(kd_t[:, :, :], kd_t[:, :, :], k_t[:, :, :], ALU.mult, qe_ready)
            dve.wait_ge(c_sq, 2)
            for t in range(TILES):
                rows = ROWS[t]
                step(dve.scalar_tensor_tensor(out=cq_n[0:rows, t, :], in0=c_sb[0:rows, t, 0:QL_R], scalar=mrs[0:rows, 0, t:t + 1],
                                              in1=g_q[0:rows, :], op0=ALU.mult, op1=ALU.mult))
                step(dve.scalar_tensor_tensor(out=ckv_n[0:rows, t, :], in0=c_sb[0:rows, t, QL_R:QL_R + KVL],
                                              scalar=mrs[0:rows, 1, t:t + 1], in1=g_kv[0:rows, :], op0=ALU.mult, op1=ALU.mult))
                cos, sin = (mixc(n)[0:rows, t * HALF:(t + 1) * HALF] for n in ("cos", "sin"))
                k1, k2 = (c_sb[0:rows, t, 384 + i:384 + i + HALF] for i in (0, HALF))
                r1, r2 = rot[0:rows, 0, 0:HALF], rot[0:rows, 1, 0:HALF]
                tt(r1, k1, cos, ALU.mult)
                tt(r2, k2, sin, ALU.mult)
                tt(kr[0:rows, t, 0:HALF], r1, r2, ALU.subtract)
                tt(r1, k1, sin, ALU.mult)
                tt(r2, k2, cos, ALU.mult)
                tt(kr[0:rows, t, HALF:], r1, r2, ALU.add, c_normed)
            dve.wait_ge(levels_zeroed, 1)
            for v in range(LEVELS):
                for j in range(2):
                    up, low = level_half(b_t[:, j, :], v, 1), level_half(b_t[:, j, :], v, 0)
                    ref = bc(low[:, :, (1 << v) - 1], 2, 1 << v)
                    dve.tensor_tensor(level_half(q_lev[:, v, j, :], v, 1), up, ref, ALU.subtract)
                    ins = dve.tensor_tensor(level_half(k_lev[:, v, j, :], v, 0), ref, low, ALU.subtract)
                    if j:
                        step(ins, lev_d)
            for v in range(LEVELS):
                dve.wait_ge(lev_e, v + 1)
                for j in range(2):
                    qh, kh = level_half(q_lev[:, v, j, :], v, 1), level_half(k_lev[:, v, j, :], v, 0)
                    dve.tensor_tensor(qh, qh, level_half(q_t[:, j, :], v, 1), ALU.mult)
                    ins = dve.tensor_tensor(kh, kh, level_half(k_t[:, j, :], v, 0), ALU.mult)
                    if j:
                        step(ins, lev_ready)
            for t in range(TILES):
                rows, n = ROWS[t], ("qr", t)
                q = banks.full(dve, n)[0:rows, 0:256].rearrange("p (h r) -> p h r", h=MH)
                cos, sin = (bc(mixc(m)[0:rows, t * HALF:(t + 1) * HALF], 1, MH) for m in ("cos", "sin"))
                q1, q2 = q[:, :, 0:HALF], q[:, :, HALF:]
                r1, r2 = (rot[0:rows, i, :].rearrange("p (h r) -> p h r", h=MH) for i in range(2))
                o = q_rot[0:rows, t, :].rearrange("p (h r) -> p h r", h=MH)
                tt(r1, q1, cos, ALU.mult)
                tt(r2, q2, sin, ALU.mult)
                tt(o[:, :, 0:HALF], r1, r2, ALU.subtract)
                tt(r1, q1, sin, ALU.mult)
                step.banked(dve.tensor_tensor(r2, q2, cos, ALU.mult), banks, n)
                tt(o[:, :, HALF:], r1, r2, ALU.add, qrot_ready)
            def sum_levels(t):
                for h in range(GH):
                    name = ("att", t, h)
                    ps = banks.full(dve, name)
                    parts_ = [(slice(0, P), 0, CHUNK, LEVELS + 1)] if t < 2 else [
                        (slice(pb, pb + n), pb % CHUNK, n, int(math.log2(n)) + 1) for tt_, pb, n in CHUNKS if tt_ == 2]
                    for i, (rows, q0, nq, nl) in enumerate(parts_):
                        lv = lambda ap: ap[rows, 0:nl * CHUNK].rearrange("p (v t) -> p v t", v=nl)[:, :, q0:q0 + nq]
                        ins = dve.tensor_tensor(lv(att_m), lv(ps), lv(mixc("gla")), ALU.mult)
                        step(ins) if i + 1 < len(parts_) else step.banked(ins, banks, name)
                    for i, (rows, q0, nq, nl) in enumerate(parts_):
                        lv = lambda ap: ap[rows, 0:nl * CHUNK].rearrange("p (v t) -> p v t", v=nl)[:, :, q0:q0 + nq]
                        step(dve.tensor_reduce(att[rows, t, h, q0:q0 + nq], lv(att_m).rearrange("p v t -> p t v"), AX.X, ALU.add),
                             att_ready if i + 1 == len(parts_) else None)

            def update_state(c):
                t, pb, n = CHUNKS[c]
                st = s_s if c == 5 else s_p
                for j in range(2):
                    name = ("u", c, j)
                    ps = banks.full(dve, name)
                    last = t * P + pb + n - 1
                    for b in range(2):
                        hp, hc = slice(64 * b, 64 * b + 64), slice(128 * b, 128 * b + 128)
                        ins = dve.scalar_tensor_tensor(out=st[hp, j, hc], in0=st[hp, j, hc], scalar=u_t[hp, j, last:last + 1],
                                                       in1=ps[hp, hc], op0=ALU.mult, op1=ALU.add)
                        step.banked(ins, banks, name) if b else step(ins)

            dve.wait_ge(state_in, 16 * GH)
            for t in range(TILES):
                sum_levels(t)
                for c in CHUNKS_BY_TILE[t]:
                    update_state(c)
            for c in range(len(CHUNKS)):
                for j in range(2):
                    banks.copied(dve, ("o", c, j))
            for t in range(TILES):
                rows = ROWS[t]
                tt(sq[0:rows, :], og[0:rows, t, :], og[0:rows, t, :], ALU.mult)
                step(dve.tensor_reduce(gss[0:rows, t * GH:(t + 1) * GH], sq[0:rows, :].rearrange("p (h n) -> p h n", h=GH),
                                       AX.X, ALU.add), gss_ready)

            def norm_out(t):
                rows = ROWS[t]
                o = og[0:rows, t, :].rearrange("p (h n) -> p h n", h=GH)
                tt(o, o, bc(grs[0:rows, t * GH:(t + 1) * GH], 2, GDV), ALU.mult)
                tt(o, o, bc(g_gla[0:rows, :], 1, GH), ALU.mult, og_ready)

            blocks = attention_blocks()

            def scores(m):
                nk, mask = blocks[m][3], blocks[m][4]
                if m >= 4:
                    banks.full(dve, ("pt", m - 4))
                ps = banks.full(dve, ("s", m))
                row = sm[:, m % 4, 0:nk]
                step.banked(dve.scalar_tensor_tensor(out=row, in0=ps[:, 0:nk], scalar=MLA_SCALE, in1=mixc(mask)[:, 0:nk],
                                                     op0=ALU.mult, op1=ALU.add), banks, ("s", m))
                step(dve.tensor_reduce(stat[:, m % 4, 0:1], row, AX.X, ALU.max))
                ts(stat[:, m % 4, 1:2], stat[:, m % 4, 0:1], -1.0, None, ALU.mult, None, mx_ready)

            def latent_out(m):
                hs, q0, nq = blocks[m][:3]
                copy(q_lat[:, hs[0]:hs[-1] + 1, q0:q0 + nq], ("ol", m), lambda ps: ps[:, 0:P].rearrange("p (h n) -> p h n", h=len(hs)))

            scores(0)
            scores(1)
            for m in range(len(blocks)):
                nk = blocks[m][3]
                dve.wait_ge(ex_ready, m + 1)
                step(dve.reciprocal(stat[:, m % 4, 3:4], stat[:, m % 4, 2:3]))
                ts(sm[:, m % 4, 0:nk], sm[:, m % 4, 0:nk], stat[:, m % 4, 3:4], None, ALU.mult, None, p_ready)
                if m + 2 < len(blocks):
                    scores(m + 2)
                if m >= 2:
                    latent_out(m - 2)
                if m == 0:
                    dve.wait_ge(grs_ready, 1)
                if m in (1, 3, 5):
                    norm_out(m // 2)
            latent_out(len(blocks) - 2)
            latent_out(len(blocks) - 1)
            for j in range(4):
                banks.copied(dve, ("r", j))
            for t in range(TILES):
                rows, n = ROWS[t], ("ogT", t)
                cols = slice(t * P, t * P + rows)
                ps = banks.full(dve, n)
                dve.tensor_tensor(o_t[:, 0:4, cols], r_t[:, :, cols], ps[:, 0:4 * rows].rearrange("p (h n) -> p h n", h=4), ALU.mult)\
                   .then_inc(banks.empty_sem(n), 1)
            for g in range(4):
                copy(o_t[:, 4 + g, 0:T_COLS], ("om", g), lambda ps: ps[:, 0:T_COLS])

            def add_mixed(t, rows):
                for c in range(2):
                    n, xr = ("mo", t, c), x[0:rows, t, c * 512:(c + 1) * 512]
                    ps = banks.full(dve, n)
                    step.banked(dve.scalar_tensor_tensor(out=xr, in0=xr, scalar=ALPHA, in1=ps[second(t, c), :],
                                                         op0=ALU.mult, op1=ALU.add), banks, n)

            layer_norm(0, add_mixed)
            for l in range(DEPTH):
                s = L[l]
                if l:
                    for c in range(1, DK_SLICES, 2):
                        copy(xt[:, c, 0:T_COLS], ("mx", c), lambda ps: ps[:, 0:T_COLS])

                    def add_pooled(t, rows):
                        for c in range(2):
                            n, cc = ("po", t, c), slice(c * 512, (c + 1) * 512)
                            ps = banks.full(dve, n)
                            step.banked(dve.tensor_tensor(acc[0:rows, t, cc], ps[0:rows, :], pool_s[0:rows, cc], ALU.mult), banks, n)
                        if t == 2:
                            dve.wait_ge(stored, 16 * (MIX_STORES + 2))
                        add_acc(t, rows)

                    dve.wait_ge(s["pool_in"], 16 * 3)

                def add_acc(t, rows):
                    step(dve.scalar_tensor_tensor(out=x[0:rows, t, :], in0=x[0:rows, t, :], scalar=ALPHA, in1=acc[0:rows, t, :],
                                                  op0=ALU.mult, op1=ALU.add))

                if l:
                    layer_norm(2, add_pooled)
                copy_xt(l + 1)
                dve.wait_ge(rbias_in, 16 * DEPTH)
                dve.wait_ge(consts_in, 16)
                banks.copied(dve, ("lg", l))
                ts(sc[:, :, :], sc[:, :, :], 1.0, None, ALU.add)
                step(dve.reciprocal(sc[:, :, :], sc[:, :, :]))
                tt(bi[:, :, :], sc[:, :, :], bc(rbias[:, l, :], 1, TILES), ALU.add)
                b4 = bi[:, :, :].rearrange("p t (g n) -> p t g n", g=NG)
                tt(g_a[:, :, :, :], b4[:, :, :, 0:4], b4[:, :, :, 4:8], ALU.max)
                tt(g_b[:, :, :, :], b4[:, :, :, 0:4], b4[:, :, :, 4:8], ALU.min)
                for w in (2, 1):
                    a0, a1 = g_a[:, :, :, 0:w], g_a[:, :, :, w:2 * w]
                    b0, b1 = g_b[:, :, :, 0:w], g_b[:, :, :, w:2 * w]
                    tt(g_c[:, :, :, 0:w], a0, a1, ALU.min)
                    tt(a0, a0, a1, ALU.max)
                    tt(b0, b0, b1, ALU.max)
                    tt(b0, b0, g_c[:, :, :, 0:w], ALU.max)
                tt(gs[:, :, :], g_a[:, :, :, 0], g_b[:, :, :, 0], ALU.add)
                for t in range(TILES):
                    other, own = bc(gs[:, t, :], 1, NG), bc(gs[:, t, :], 2, NG)
                    tt(cmp1[:, t, :, :], other, own, ALU.is_gt)
                    tt(cmp2[:, t, :, :], other, own, ALU.is_equal)
                    tt(cmp2[:, t, :, :], cmp2[:, t, :, :], const("lower_group").rearrange("p (g n) -> p g n", g=NG), ALU.mult)
                tt(cmp1[:, :, :, :], cmp1[:, :, :, :], cmp2[:, :, :, :], ALU.add)
                step(dve.tensor_reduce(rank[:, :, :], cmp1[:, :, :, :], AX.X, ALU.add))
                ts(rank[:, :, :], rank[:, :, :], float(TOPG), None, ALU.is_lt)
                m4 = mk[:, :, :].rearrange("p t (g n) -> p t g n", g=NG)
                tt(m4, b4, bc(rank[:, :, :], 3, E // NG), ALU.mult)
                ts(rank[:, :, :], rank[:, :, :], 1.0, BIG, ALU.subtract, ALU.mult)
                tt(m4, m4, bc(rank[:, :, :], 3, E // NG), ALU.add)
                for t in range(TILES):
                    step(dve.max(mx8[:, t, :], mk[:, t, :]))
                    step(dve.match_replace(mr[:, t, :], in_to_replace=mx8[:, t, :], in_values=mk[:, t, :], imm_value=-BIG))
                tt(sel[:, :, :], mr[:, :, :], mk[:, :, :], ALU.not_equal)
                tt(tmp[:, :, :], sc[:, :, :], sel[:, :, :], ALU.mult)
                step(dve.tensor_reduce(wsum[:, :], tmp[:, :, :], AX.X, ALU.add))
                step(dve.reciprocal(wsum[:, :], wsum[:, :]))
                ts(wsum[:, :], wsum[:, :], ROUTED_SCALE, None, ALU.mult)
                tt(wt_x[:, :, 0:E], tmp[:, :, :], bc(wsum[:, :], 2, E), ALU.mult)
                valid = bc(const("valid"), 2, E)
                tt(wt_x[:, :, 0:E], wt_x[:, :, 0:E], valid, ALU.mult)
                step(dve.tensor_copy(wt_x[:, :, E:], wt_x[:, :, 0:4]))
                tt(sel[:, :, :], sel[:, :, :], valid, ALU.mult, s["sel_ready"])
                for b in range(2):
                    n = ("su", l, b)
                    ps = banks.full(dve, n)
                    banks.copied(dve, ("sg", l, b))
                    dve.tensor_tensor(sh_h[:, b, :], sh_sg[:, b, :], ps[:, 0:T_COLS], ALU.mult).then_inc(banks.empty_sem(n), 1)
                n = ("pos", l)
                ps = banks.full(dve, n)
                ps3 = ps[:, 0:TILES * E].rearrange("p (t e) -> p t e", t=TILES)
                step(dve.tensor_scalar(pos_x[:, :, 0:E], ps3, 1.0, None, ALU.add))
                step.banked(dve.tensor_copy(cnt[:, :], ps[:, TILES * E:(TILES + 1) * E]), banks, n)
                tt(pos_x[:, :, 0:E], pos_x[:, :, 0:E], sel[:, :, :], ALU.mult)
                ts(pos_x[:, :, 0:E], pos_x[:, :, 0:E], -1.0, None, ALU.add)
                ts(pos_x[:, :, E:], pos_x[:, :, 0:4], -float(SLOTS), None, ALU.add)
                step(dve.tensor_copy(pos_x[64:128, 2, :], pos_x[0:64, 2, :]))
                step(dve.tensor_reduce(cmax[:, :], cnt[:, :], AX.X, ALU.max))
                ts(thr_c[:, :], const("thr"), cmax[:, 0:1], None, ALU.is_lt)
                step(dve.tensor_reduce(cmax[:, :], thr_c[:, :], AX.X, ALU.add))
                ts(n_rounds[:, :], cmax[:, :], 1.0, None, ALU.add, None, s["rounds_ready"])
                dve.wait_ge(s["x_split"], 1)
                dve.tensor_tensor(xl[:, 0:2, :], x[:, 0:2, :], xh[:, 0:2, :].bitcast(F32), ALU.subtract)
                dve.tensor_tensor(xh[64:128, 2, :], x[0:64, 2, :], xh[0:64, 2, :].bitcast(F32), ALU.subtract).then_inc(s["x_split"], 1)
                for t in range(TILES):
                    rows = ROWS[t]
                    copy(acc[0:rows, t, 512:D], ("sd", l, t, 1), lambda ps: ps[second(t, 1), :])
                dve_experts(dve, l, step)
                layer_norm(2 * l + 1, add_acc)


_OUTS = [("y_prompt", (1, SEQ, D)), ("y_sample", (1, N_DEC, D)),
         ("prompt_ckv", (1, N_PROMPT, KVL)), ("prompt_krope", (1, N_PROMPT, ROPE)),
         ("prompt_gla_state", (1, GH, GDK, GDV)), ("prompt_pool_rows", (1, 15, D)),
         ("sample_ckv", (1, N_DEC, KVL)), ("sample_krope", (1, N_DEC, ROPE)),
         ("sample_gla_state", (1, GH, GDK, GDV)), ("sample_pool_rows", (1, 15, D))]


def kernel(**inputs):
    import concourse.bacc as _bacc
    from concourse.bass_utils import run_bass_kernel_spmd as _run

    nc = _bacc.Bacc("TRN2", target_bir_lowering=False, num_devices=1)
    tables = dict(zip(("cst", "mix", "band"), constants()))
    arrays, a = {}, {}
    for name, v in {**inputs, **tables}.items():
        v = np.ascontiguousarray(v)
        arrays[f"in_{name}_dram"] = v
        a[name] = nc.dram_tensor(f"in_{name}_dram", v.shape, mybir.dt.from_np(v.dtype), kind="ExternalInput").ap()
    a["outs"] = {n: nc.dram_tensor(f"out_{n}_dram", shape, F32, kind="ExternalOutput").ap() for n, shape in _OUTS}
    build(nc, a)
    r = _run(nc, [arrays], core_ids=[0])
    return tuple(r.results[0][f"out_{n}_dram"] for n, _ in _OUTS)
```
